# Optimizing a Trainium2 kernel written in Bass

```python
import math
import jax, jax.numpy as jnp
from jax import lax
import numpy as np

D_MODEL = 2048
BATCH = 1
SEQ = 512
DEPTH = 1

N_Q_HEADS = 32
N_KV_HEADS = 4
HEAD_DIM = 64
Q_PER_KV = N_Q_HEADS // N_KV_HEADS
WINDOW = 128
BLOCK = 128
ATTN_WIDTH = N_Q_HEADS * HEAD_DIM
KV_WIDTH = N_KV_HEADS * HEAD_DIM

CONV_WIDTH = D_MODEL
CONV_K = 3

N_BRANCHES = 2

Q_OFF = 0
K_OFF = Q_OFF + ATTN_WIDTH
V_OFF = K_OFF + KV_WIDTH
CB_OFF = V_OFF + KV_WIDTH
CC_OFF = CB_OFF + CONV_WIDTH
CH_OFF = CC_OFF + CONV_WIDTH
G_OFF = CH_OFF + CONV_WIDTH
IN_WIDTH = G_OFF + N_BRANCHES * D_MODEL

PEER_HEADS = 8
PEER_N_KEYS = 128
PEER_N_EXPERTS = PEER_N_KEYS * PEER_N_KEYS
PEER_TOPK = 16
PEER_QDIM = 256
PEER_HALF = PEER_QDIM // 2
PEER_CHUNK = 128

LN_EPS = 1e-5
ALPHA = (2.0 * DEPTH) ** 0.25
BETA = (8.0 * DEPTH) ** -0.25

kernel_name = "hybrid_swa_sink_shortconv_peer_deepnorm"

def layer_norm(x, g, b):
    xf = x.astype(jnp.float32)
    mu = jnp.mean(xf, axis=-1, keepdims=True)
    var = jnp.mean(jnp.square(xf - mu), axis=-1, keepdims=True)
    y = (xf - mu) * lax.rsqrt(var + LN_EPS) * g.astype(jnp.float32) + b.astype(jnp.float32)
    return y.astype(x.dtype)

def sliding_window_sink_attention(q, k, v, sinks):
    b_, s_ = q.shape[0], q.shape[1]
    nb = s_ // BLOCK
    qb = q.reshape(b_, nb, BLOCK, N_KV_HEADS, Q_PER_KV, HEAD_DIM)
    kb = k.reshape(b_, nb, BLOCK, N_KV_HEADS, HEAD_DIM)
    vb = v.reshape(b_, nb, BLOCK, N_KV_HEADS, HEAD_DIM)

    def with_prev(t):
        prev = jnp.pad(t, ((0, 0), (1, 0), (0, 0), (0, 0), (0, 0)))[:, :-1]
        return jnp.concatenate([prev, t], axis=2)

    kw = with_prev(kb)
    vw = with_prev(vb)
    scores = jnp.einsum('bnqhgd,bnkhd->bnhgqk', qb, kw).astype(jnp.float32) * (HEAD_DIM ** -0.5)

    qi = jnp.arange(BLOCK)[:, None]
    kj = jnp.arange(2 * BLOCK)[None, :]
    rel = BLOCK + qi - kj
    band = (rel >= 0) & (rel < WINDOW)
    kpos = jnp.arange(nb)[:, None] * BLOCK - BLOCK + kj
    mask = band[None] & (kpos >= 0)[:, None, :]
    scores = jnp.where(mask[None, :, None, None], scores, -jnp.inf)

    sink = sinks.astype(jnp.float32).reshape(N_KV_HEADS, Q_PER_KV)[None, None, :, :, None, None]
    m = jnp.maximum(jnp.max(scores, axis=-1, keepdims=True), sink)
    p = jnp.exp(scores - m)
    denom = jnp.sum(p, axis=-1, keepdims=True) + jnp.exp(sink - m)
    probs = (p / denom).astype(v.dtype)
    out = jnp.einsum('bnhgqk,bnkhd->bnqhgd', probs, vw)
    return out.reshape(b_, s_, ATTN_WIDTH)

def causal_short_conv(u, w):
    return lax.conv_general_dilated(
        u, w[:, None, :].astype(u.dtype), window_strides=(1,), padding=[(CONV_K - 1, 0)],
        dimension_numbers=('NWC', 'WIO', 'NWC'), feature_group_count=u.shape[-1])

def peer_ffn(x, w_q, sub_keys, u_tab, v_tab):
    b_, s_, d_ = x.shape
    t_ = b_ * s_
    xt = x.reshape(t_, d_)
    q = (xt @ w_q).reshape(t_, PEER_HEADS, 2, PEER_HALF)
    s = jnp.einsum('thpc,hpnc->thpn', q, sub_keys).astype(jnp.float32)
    top_s, top_i = lax.top_k(s, PEER_TOPK)
    cand_s = top_s[:, :, 0, :, None] + top_s[:, :, 1, None, :]
    cand_i = top_i[:, :, 0, :, None] * PEER_N_KEYS + top_i[:, :, 1, None, :]
    cand_s = cand_s.reshape(t_, PEER_HEADS, PEER_TOPK * PEER_TOPK)
    cand_i = cand_i.reshape(t_, PEER_HEADS, PEER_TOPK * PEER_TOPK)
    best_s, best_pos = lax.top_k(cand_s, PEER_TOPK)
    expert = jnp.take_along_axis(cand_i, best_pos, axis=-1)
    gate = jax.nn.softmax(best_s, axis=-1)

    nc = t_ // PEER_CHUNK

    def per_block(args):
        xc, ec, gc = args
        u = jnp.take(u_tab, ec, axis=0)
        act = jax.nn.gelu(jnp.einsum('cd,chkd->chk', xc, u).astype(jnp.float32), approximate=False)
        wgt = (gc * act).astype(xc.dtype)
        v = jnp.take(v_tab, ec, axis=0)
        return jnp.einsum('chk,chkd->cd', wgt, v)

    y = lax.map(per_block, (xt.reshape(nc, PEER_CHUNK, d_),
                            expert.reshape(nc, PEER_CHUNK, PEER_HEADS, PEER_TOPK),
                            gate.reshape(nc, PEER_CHUNK, PEER_HEADS, PEER_TOPK)))
    return y.reshape(b_, s_, d_)

def setup_inputs(seed: int = 0) -> dict:
    key = jax.random.key(seed)
    ks = jax.random.split(key, 17)
    f32 = jnp.float32
    nrm = lambda k, shape, scale: jax.random.normal(k, shape, f32) * scale
    x = jax.random.normal(ks[0], (BATCH, SEQ, D_MODEL), f32)
    w_in = nrm(ks[1], (DEPTH, D_MODEL, IN_WIDTH), D_MODEL ** -0.5)
    b_gate = nrm(ks[2], (DEPTH, N_BRANCHES * D_MODEL), 0.02)
    sinks = nrm(ks[3], (DEPTH, N_Q_HEADS), 0.5)
    conv_w = nrm(ks[4], (DEPTH, CONV_K, CONV_WIDTH), CONV_K ** -0.5)
    w_attn_out = nrm(ks[5], (DEPTH, ATTN_WIDTH, D_MODEL), ATTN_WIDTH ** -0.5)
    w_conv_out = nrm(ks[6], (DEPTH, CONV_WIDTH, D_MODEL), CONV_WIDTH ** -0.5)
    w_o = nrm(ks[7], (DEPTH, D_MODEL, D_MODEL), BETA * D_MODEL ** -0.5)
    ln1_g = 1.0 + nrm(ks[8], (DEPTH, D_MODEL), 0.02)
    ln1_b = nrm(ks[9], (DEPTH, D_MODEL), 0.02)
    peer_w_q = nrm(ks[10], (DEPTH, D_MODEL, PEER_HEADS * PEER_QDIM), D_MODEL ** -0.5)
    peer_sub_keys = nrm(ks[11], (DEPTH, PEER_HEADS, 2, PEER_N_KEYS, PEER_HALF), PEER_HALF ** -0.5)
    peer_u = nrm(ks[12], (DEPTH, PEER_N_EXPERTS, D_MODEL), D_MODEL ** -0.5)
    peer_v = nrm(ks[13], (DEPTH, PEER_N_EXPERTS, D_MODEL), BETA)
    ln2_g = 1.0 + nrm(ks[14], (DEPTH, D_MODEL), 0.02)
    ln2_b = nrm(ks[15], (DEPTH, D_MODEL), 0.02)
    return {"x": x, "w_in": w_in, "b_gate": b_gate, "sinks": sinks, "conv_w": conv_w,
            "w_attn_out": w_attn_out, "w_conv_out": w_conv_out, "w_o": w_o,
            "ln1_g": ln1_g, "ln1_b": ln1_b, "peer_w_q": peer_w_q, "peer_sub_keys": peer_sub_keys,
            "peer_u": peer_u, "peer_v": peer_v, "ln2_g": ln2_g, "ln2_b": ln2_b}

def reference(x, w_in, b_gate, sinks, conv_w, w_attn_out, w_conv_out, w_o, ln1_g, ln1_b,
              peer_w_q, peer_sub_keys, peer_u, peer_v, ln2_g, ln2_b):
    b_, s_ = x.shape[0], x.shape[1]
    h = x
    for l in range(DEPTH):
        z = h @ w_in[l]
        q = z[..., Q_OFF:K_OFF].reshape(b_, s_, N_Q_HEADS, HEAD_DIM)
        k = z[..., K_OFF:V_OFF].reshape(b_, s_, N_KV_HEADS, HEAD_DIM)
        v = z[..., V_OFF:CB_OFF].reshape(b_, s_, N_KV_HEADS, HEAD_DIM)
        cb = z[..., CB_OFF:CC_OFF]
        cc = z[..., CC_OFF:CH_OFF]
        ch = z[..., CH_OFF:G_OFF]
        gates = jax.nn.sigmoid((z[..., G_OFF:] + b_gate[l]).astype(jnp.float32)).astype(h.dtype)

        attn = sliding_window_sink_attention(q, k, v, sinks[l]) @ w_attn_out[l]
        conv = (cb * causal_short_conv(cc * ch, conv_w[l])) @ w_conv_out[l]
        merged = gates[..., :D_MODEL] * attn + gates[..., D_MODEL:] * conv
        mixed = merged @ w_o[l]
        h = layer_norm(ALPHA * h + mixed, ln1_g[l], ln1_b[l])

        ffn = peer_ffn(h, peer_w_q[l], peer_sub_keys[l], peer_u[l], peer_v[l])
        h = layer_norm(ALPHA * h + ffn, ln2_g[l], ln2_b[l])
    return h


_drawn_inputs = setup_inputs


def setup_inputs(seed=0):
    import zlib

    import numpy as np

    out = dict(_drawn_inputs(seed))
    spreads = {}
    factors = {'b_gate': 4.781, 'sinks': 8.0, 'ln2_g': 2.788, 'ln2_b': 2.75}
    for name, (base, spread) in spreads.items():
        noise = np.random.default_rng([zlib.crc32(name.encode()), seed]).standard_normal(out[name].shape)
        drawn = base * np.exp(spread * noise) if base else spread * noise
        out[name] = __import__('jax').numpy.asarray(drawn.astype(out[name].dtype))
    for name, factor in factors.items():
        out[name] = (out[name] * factor).astype(out[name].dtype)
    return out
```

```python
import concourse.bass as bass
from concourse import mybir
from contextlib import ExitStack

F32 = mybir.dt.float32
U32 = mybir.dt.uint32
ALU = mybir.AluOpType
ACT = mybir.ActivationFunctionType
AX = mybir.AxisListType

P = 128
D = 2048
SEQ = 512
HALF = 256
TILES = HALF // P
HALVES = SEQ // HALF
KT = D // P
HD = 64
HEADS = 32
KV_HEADS = 4
EPS = 1e-5
ALPHA = 2.0 ** 0.25
NEG = -1e30
LOWEST = -3.4e38

UC = 256
K_OFF = HEADS * HD
V_OFF = K_OFF + KV_HEADS * HD
CB_OFF = V_OFF + KV_HEADS * HD
CC_OFF = CB_OFF + D
CH_OFF = CC_OFF + D
G_OFF = CH_OFF + D

ORDER = (0, 2, 1, 3)
U_K = 0
U_V = 2
U_Q = 3
U_CONV = 11
U_GATE = 35
U_OUT = 67
U_PQ = 75
UNITS = 83

PH = 8
NK = 128
TOPK = 16
SLOTS = PH * TOPK
ROWS = 2 * SLOTS
RING = 4
OVERLAP = True
START = 32


def build(nc, x, w_in, b_gate, sinks, conv_w, w_attn_out, w_conv_out, w_o, ln1_g, ln1_b,
          peer_w_q, peer_sub_keys, peer_u, peer_v, ln2_g, ln2_b, out):
    ctx = ExitStack()
    with ctx:
        def sb(name, shape, dt=F32):
            return ctx.enter_context(nc.sbuf_tensor(name, shape, dt))

        def sem(name):
            return ctx.enter_context(nc.semaphore(name))

        wbuf = [sb(f"wbuf{i}", [P, KT, UC]) for i in range(2)]
        xT = sb("xT", [P, KT, HALF])
        aT = sb("aT", [P, KT, HALF])
        cT = sb("cT", [P, KT, HALF])
        mT = sb("mT", [P, KT, HALF])
        h0 = sb("h0", [P, TILES, D])
        row = [sb(f"row{i}", [P, D]) for i in range(RING)]
        y = sb("y", [P, D])
        ln2 = sb("ln2", [P, 2, D])
        kT = sb("kT", [P, KV_HEADS, P + HALF])
        v = sb("v", [P, 1 + TILES, KV_HEADS * HD])
        stage = [sb(f"stage{i}", [P, 2, HALF]) for i in range(4)]
        uconv = sb("uconv", [P, 2, 2 + HALF])
        carry = sb("carry", [P, KT, 2])
        skT = sb("skT", [P, 2 * PH, NK])
        mask = sb("mask", [P, 2, 2 * P])
        ident = sb("ident", [P, P])
        vecs = sb("vecs", [P, 80])
        sink = sb("sink", [P, HEADS])
        nsink = sb("nsink", [P, HEADS])
        eps = sb("eps", [P, 1])
        iota = sb("iota", [P, TOPK])
        nmax = sb("nmax", [P, 4])
        nmx = sb("nmx", [P, 4])
        sarg = sb("sarg", [P, 4])
        esink = sb("esink", [P, 4])
        rowsum = sb("rowsum", [P, 4])
        den = sb("den", [P, 4])
        rden = sb("rden", [P, 4])
        bst = sb("bst", [P, TILES, 4, 6])
        mv = sb("mv", [P, TILES, 2])
        sd = sb("sd", [P, TILES])
        rstd = sb("rstd", [P, TILES])
        bst2 = sb("bst2", [P, 4, 6])
        mv2 = sb("mv2", [P, 2])
        sd2 = sb("sd2", [P, 1])
        rstd2 = sb("rstd2", [P, 1])
        gmax = sb("gmax", [P, TILES, PH])
        gsum = sb("gsum", [P, TILES, PH])
        grec = sb("grec", [P, TILES, PH])
        expert = sb("expert", [P, HALVES, TILES, SLOTS], U32)
        gate = sb("gate", [P, HALVES, TILES, SLOTS])
        cols = sb("cols", [P, 2, 16], U32)
        dots = sb("dots", [P, SLOTS])
        gelu = sb("gelu", [P, SLOTS])
        wgt = sb("wgt", [P, SLOTS])

        mflat = mT[:, :, :].rearrange("p k t -> p (k t)")

        def scratch(at, n):
            return mflat[:, at:at + n]

        sm = scratch(0, 1024).rearrange("p (h k) -> p h k", h=4)
        probs = scratch(1024, 1024).rearrange("p (h k) -> p h k", h=4)
        pT = scratch(2048, 1024).rearrange("p (h k) -> p h k", h=4)
        attn = scratch(3072, 256)
        keys = scratch(3328, 768).rearrange("p (n k) -> p n k", n=2)
        ks = scratch(0, 1024).rearrange("p (n t a k) -> p n t a k", n=2, t=2, a=2)
        ksw = scratch(1024, 512).rearrange("p (t a k) -> p t a k", t=2, a=2)
        cand = scratch(1536, 512).rearrange("p (t k) -> p t k", t=2)
        candw = scratch(2048, 512).rearrange("p (t k) -> p t k", t=2)
        tops = scratch(2560, 64).rearrange("p (t a k) -> p t a k", t=2, a=2)
        topi = scratch(2624, 64).bitcast(U32).rearrange("p (t a k) -> p t a k", t=2, a=2)
        bests = scratch(2688, 32).rearrange("p (t k) -> p t k", t=2)
        bestp = scratch(2720, 32).bitcast(U32).rearrange("p (t k) -> p t k", t=2)
        posab = scratch(2752, 64).bitcast(U32).rearrange("p (t a k) -> p t a k", t=2, a=2)
        onehot = scratch(0, 2048).rearrange("p (h s a) -> p h s a", h=PH, s=TOPK)
        best = scratch(3840, 256).rearrange("p (t h k) -> p t h k", t=TILES, h=PH)
        found = scratch(2816, 1024).rearrange("p (t h k) -> p t h k", t=TILES, h=PH)
        key0 = scratch(2048, SLOTS)
        key1 = scratch(2176, SLOTS)
        vecs_in = mflat[0:80, 3072:3072 + P]
        subk = mflat[:, 0:2048].rearrange("p (g c) -> p g c", g=2 * PH)
        ln1 = aT[:, :, :].rearrange("p k t -> p (k t)").rearrange("p (a d) -> p a d", a=2)
        h1 = cT[:, :, :].rearrange("p k t -> p (k t)").rearrange("p (t d) -> p t d", t=TILES)
        hs = [h0[:, :, :], h1]

        dense_ps = [ctx.enter_context(nc.psum_tensor(f"dense_ps{i}", [P, 2, HALF], F32)) for i in range(4)]
        score_ps = [ctx.enter_context(nc.psum_tensor(f"score_ps{i}", [P, 2, 2 * P], F32)) for i in range(2)]
        oT_ps = ctx.enter_context(nc.psum_tensor("oT_ps", [P, 2 * P], F32))
        o_ps = ctx.enter_context(nc.psum_tensor("o_ps", [P, 4, HD], F32))

        w_ready = [sem(f"w_ready{i}") for i in range(2)]
        k_ready = [sem(f"k_ready{u}") for u in range(2)]
        small_in = sem("small_in")
        x_in = sem("x_in")
        xres_in = sem("xres_in")
        ln1_in = sem("ln1_in")
        masks_ok = sem("masks_ok")
        const_ok = sem("const_ok")
        nsink_ok = sem("nsink_ok")
        setup_ready = sem("setup_ready")
        setup_done = sem("setup_done")
        tr_ready = sem("tr_ready")
        tr_done = sem("tr_done")
        dense_ready = sem("dense_ready")
        dense_out = sem("dense_out")
        kv_shift = sem("kv_shift")
        keys_ready = sem("keys_ready")
        scores_ready = sem("scores_ready")
        masked = sem("masked")
        nmax_ready = sem("nmax_ready")
        sarg_ready = sem("sarg_ready")
        exp_done = sem("exp_done")
        esink_ready = sem("esink_ready")
        den_ready = sem("den_ready")
        rden_ready = sem("rden_ready")
        pT_ready = sem("pT_ready")
        pT_copied = sem("pT_copied")
        o_ready = sem("o_ready")
        attn_ready = sem("attn_ready")
        oT_ready = sem("oT_ready")
        aT_done = sem("aT_done")
        conv_step = sem("conv_step")
        gate_step = sem("gate_step")
        out_step = sem("out_step")
        stats_step = sem("stats_step")
        sd_ready = sem("sd_ready")
        ln_step = sem("ln_step")
        h_ready = sem("h_ready")
        ks_ready = sem("ks_ready")
        ks_out = sem("ks_out")
        pick_step = sem("pick_step")
        gather_step = sem("gather_step")
        gexp_ready = sem("gexp_ready")
        gate_norm = sem("gate_norm")
        expert_ready = sem("expert_ready")
        cols_ready = sem("cols_ready")
        row_in = [sem(f"row_in{i}") for i in range(RING)]
        row_used = sem("row_used")
        gelu_ready = sem("gelu_ready")
        y_init = sem("y_init")
        wgt_ready = sem("wgt_ready")
        fin_step = sem("fin_step")
        sd2_ready = sem("sd2_ready")
        out_sent = sem("out_sent")

        went_on = sem("went_on")

        block = ctx.enter_context(nc.Block())

        w_in_v = w_in.rearrange("l (k p) n -> p (l k) n", p=P)
        wa_v = w_attn_out.rearrange("l (k p) n -> p (l k) n", p=P)
        wc_v = w_conv_out.rearrange("l (k p) n -> p (l k) n", p=P)
        wo_v = w_o.rearrange("l (k p) n -> p (l k) n", p=P)
        wq_v = peer_w_q.rearrange("l (k p) n -> p (l k) n", p=P)
        x_v = x.rearrange("b (t p) d -> p (b t) d", p=P)
        out_v = out.rearrange("b (t p) d -> p (b t) d", p=P)
        u_tab = peer_u.rearrange("l e d -> (l e) d")
        v_tab = peer_v.rearrange("l e d -> (l e) d")

        @block.sync
        def _(sp):
            sp.dma_start(h0[:, :, :], x_v[:, 0:TILES, :]).then_inc(x_in, 16)
            sp.dma_start(vecs_in[0:32, :], b_gate.rearrange("l (c p) -> (l c) p", p=P)).then_inc(small_in, 16)
            sp.dma_start(vecs_in[32:80, :], conv_w.rearrange("l w (c p) -> (l w c) p", p=P)).then_inc(small_in, 16)
            sp.dma_start(sink[:, :], sinks[0, :].partition_broadcast(P)).then_inc(small_in, 16)
            sp.dma_start(subk, peer_sub_keys.rearrange("l h a n c -> n (l h a) c")).then_inc(small_in, 16)
            sp.dma_start(ln2[:, 0, :], ln2_g[0, :].partition_broadcast(P)).then_inc(small_in, 16)
            sp.dma_start(ln2[:, 1, :], ln2_b[0, :].partition_broadcast(P)).then_inc(small_in, 16)

            def load(n, slot, src, col):
                sp.wait_ge(dense_ready, n - 1)
                sp.sem_inc(went_on, 1)
                sp.dma_start(wbuf[slot][:, :, :], src[:, :, bass.ds(col, UC)]).then_inc(w_ready[slot], 16)

            for b in range(HALVES):
                n0 = UNITS * b
                if b:
                    sp.wait_ge(dense_ready, U_OUT)
                    sp.dma_start(h1, x_v[:, TILES:2 * TILES, :]).then_inc(x_in, 16)
                for u in range(2):
                    n = n0 + U_K + u
                    if n >= 2:
                        sp.wait_ge(dense_ready, n - 1)
                    for c in range(2):
                        for twice in range(2):
                            col = K_OFF + (2 * u + c) * HD
                            sp.dma_start(wbuf[n % 2][:, :, c * P + twice * HD:c * P + (twice + 1) * HD],
                                         w_in_v[:, :, col:col + HD]).then_inc(k_ready[u], 16)
                load(n0 + U_V, (n0 + U_V) % 2, w_in_v, V_OFF)
                with sp.Fori(0, 4) as i:
                    for c in range(2):
                        n = n0 + U_Q + c
                        load(n + 2 * i, n % 2, w_in_v, i * (2 * UC) + c * UC)
                with sp.Fori(0, 4) as i:
                    for c in range(6):
                        n = n0 + U_CONV + c
                        load(n + 6 * i, n % 2, w_in_v, i * (2 * UC) + (CB_OFF + (c % 3) * D + (c // 3) * UC))
                with sp.Fori(0, 8) as i:
                    for c, (src, col) in enumerate(((w_in_v, G_OFF), (w_in_v, G_OFF + D), (wa_v, 0), (wc_v, 0))):
                        n = n0 + U_GATE + c
                        load(n + 4 * i, n % 2, src, i * UC + col)
                sp.wait_ge(dense_ready, n0 + U_OUT)
                sp.dma_start(ln1[:, 0, :], ln1_g[0, :].partition_broadcast(P)).then_inc(ln1_in, 16)
                sp.dma_start(ln1[:, 1, :], ln1_b[0, :].partition_broadcast(P)).then_inc(ln1_in, 16)
                if b:
                    sp.dma_start(h1, x_v[:, TILES:2 * TILES, :]).then_inc(xres_in, 16)
                for base, src in ((U_OUT, wo_v), (U_PQ, wq_v)):
                    with sp.Fori(0, 4) as i:
                        for c in range(2):
                            n = n0 + base + c
                            load(n + 2 * i, n % 2, src, i * (2 * UC) + c * UC)

        @block.gpsimd
        def _(pool):
            pool.memset(ident[:, :], 0.0).then_inc(masks_ok, 1)
            pool.memset(mask[:, :, :], 0.0).then_inc(masks_ok, 1)
            pool.iota(iota[:, :], [[1, TOPK]], base=0, channel_multiplier=0,
                      allow_small_or_imprecise_dtypes=True).then_inc(masks_ok, 1)
            pool.wait_ge(masks_ok, 3)
            pool.affine_select(out=ident[:, :], in_=ident[:, :], compare_op=ALU.not_equal, fill=1.0,
                               base=0, pattern=[[-1, P]], channel_multiplier=1).then_inc(masks_ok, 1)
            pool.affine_select(out=mask[:, :, :], in_=mask[:, :, :], compare_op=ALU.is_gt, fill=NEG,
                               base=0, pattern=[[0, 2], [1, 2 * P]], channel_multiplier=-1).then_inc(masks_ok, 1)
            pool.wait_ge(masks_ok, 5)
            pool.affine_select(out=mask[:, :, :], in_=mask[:, :, :], compare_op=ALU.is_ge, fill=NEG,
                               base=P, pattern=[[0, 2], [-1, 2 * P]], channel_multiplier=1).then_inc(masks_ok, 1)
            pool.wait_ge(masks_ok, 6)
            pool.memset(mask[:, 0, 0:P], NEG).then_inc(masks_ok, 1)

            for t in range(HALVES * TILES):
                b = t // TILES
                if t % TILES == 0:
                    pool.wait_ge(expert_ready, 2 * (b + 1))
                for part, tab in ((0, u_tab), (1, v_tab)):
                    row0 = t * ROWS + part * SLOTS
                    with pool.Fori(0, 4) as i:
                        for c in range(2):
                            pool.wait_ge(row_used, 32 * i + (row0 - 16 + 16 * c + START))
                            nc.gpsimd.tensor_copy(cols[:, c, :], expert[:, b, t % TILES, bass.ds(i * 32 + 16 * c, 16)]
                                                  ).then_inc(cols_ready, 1)
                            pool.wait_ge(cols_ready, 2 * i + (row0 // 16 + c + 1))
                            for j in range(16):
                                g = row0 + 16 * c + j
                                pool.wait_ge(row_used, 32 * i + (g - RING + 1 + START))
                                pool.sem_inc(went_on, 1)
                                pool.indirect_dma_start(
                                    out=row[j % RING][:, :], out_offset=None, in_=tab[:, :],
                                    in_offset=bass.IndirectOffsetOnAxis(ap=cols[:, c, j:j + 1], axis=0),
                                ).then_inc(row_in[j % RING], 16)

        @block.scalar
        def _(act):
            def move_setup():
                act.wait_ge(setup_ready, 1)
                act.activation(vecs[:, :], oT_ps[:, 0:80], ACT.Copy).then_inc(setup_done, 1)
                for q in range(4):
                    act.wait_ge(setup_ready, 2 + q)
                    act.activation(skT[:, 4 * q:4 * q + 4, :].rearrange("p g n -> p (g n)"),
                                   dense_ps[q][:, :, :].rearrange("p c t -> p (c t)"), ACT.Copy).then_inc(setup_done, 1)

            def move_transposes(call):
                for r in range(8):
                    act.wait_ge(tr_ready, 8 * call + r + 1)
                    act.activation(xT[:, 2 * r:2 * r + 2, :].rearrange("p k t -> p (k t)"),
                                   score_ps[r % 2][:, :, :].rearrange("p k t -> p (k t)"), ACT.Copy).then_inc(tr_done, 1)

            def peer_tile(t, stage_of):
                if "u" in stage_of:
                    act.wait_ge(row_used, ROWS * t + SLOTS + START)
                    act.activation(gelu[:, :], dots[:, :], ACT.Gelu).then_inc(gelu_ready, 1)
                    if t:
                        act.wait_ge(out_sent, 16 * t)
                    act.activation(y[:, :], hs[t // TILES][:, t % TILES, :], ACT.Copy, scale=ALPHA).then_inc(y_init, 1)
                if "v" in stage_of:
                    act.wait_ge(fin_step, 9 * t + 5)
                    act.activation(sd2[:, :], mv2[:, 1:2], ACT.Sqrt, bias=eps[:, :]).then_inc(sd2_ready, 1)
                    act.wait_ge(fin_step, 9 * (t + 1))
                    act.dma_start(out_v[:, t, :], y[:, :]).then_inc(out_sent, 16)

            move_setup()
            for b in range(HALVES):
                n0 = UNITS * b
                with_rows = b == 1 and OVERLAP
                move_transposes(2 * b)
                if b:
                    act.wait_ge(dense_ready, n0 + 1)
                    act.activation(kT[:, :, 0:P], kT[:, :, HALF:HALF + P], ACT.Copy).then_inc(kv_shift, 1)
                    act.activation(v[:, 0, :], v[:, TILES, :], ACT.Copy).then_inc(kv_shift, 1)
                    act.wait_ge(kv_shift, 2)
                else:
                    act.wait_ge(const_ok, 1)
                for u in range(2):
                    n = n0 + U_K + u
                    act.wait_ge(dense_ready, n + 1)
                    act.activation(kT[:, 2 * u:2 * u + 2, P:P + HALF], dense_ps[n % 4][:, :, :], ACT.Copy
                                   ).then_inc(dense_out, 1)
                n = n0 + U_V
                act.wait_ge(dense_ready, n + 1)
                act.activation(v[:, 1:1 + TILES, :], dense_ps[n % 4][:, :, :], ACT.Copy).then_inc(dense_out, 1)

                act.wait_ge(dense_out, n + 1)
                if not b:
                    act.wait_ge(setup_done, 5)

                if b:
                    act.wait_ge(expert_ready, TILES * b)

                s0 = 16 * b
                with act.Fori(0, 2) as i:
                    for u in range(4):
                        n = n0 + U_Q + u
                        if u % 2 == 0:
                            act.activation(keys[:, u // 2, :],
                                           kT[:, bass.ds(2 * i + u // 2, 1), :].rearrange("p o k -> p (o k)"),
                                           ACT.Copy).then_inc(keys_ready, 1)
                        act.wait_ge(dense_ready, 4 * i + (n + 1))
                        act.activation(stage[n % 4][:, :, :], dense_ps[n % 4][:, :, :], ACT.Copy).then_inc(dense_out, 1)
                        for t in range(TILES):
                            s = s0 + 2 * u + t
                            act.wait_ge(nmax_ready, 8 * i + (s + 1))
                            for h in ORDER:
                                act.activation(probs[:, h, :], sm[:, h, :], ACT.Exp, bias=nmx[:, h:h + 1], scale=-1.0,
                                               accum_out=rowsum[:, h:h + 1]).then_inc(exp_done, 1)
                            act.wait_ge(sarg_ready, 8 * i + (s + 1))
                            act.activation(esink[:, :], sarg[:, :], ACT.Exp).then_inc(esink_ready, 1)
                            for a in range(2):
                                act.wait_ge(pT_ready, 16 * i + (2 * s + a + 1))
                                act.activation(pT[:, 2 * a:2 * a + 2, :], score_ps[a][:, :, :], ACT.Copy
                                               ).then_inc(pT_copied, 1)
                            act.wait_ge(oT_ready, 8 * i + (s + 1 + START))
                            act.activation(aT[:, bass.ds(8 * i + 2 * u, 2), t * P:(t + 1) * P],
                                           oT_ps[:, :].rearrange("p (c t) -> p c t", c=2), ACT.Copy).then_inc(aT_done, 1)
                if with_rows:
                    peer_tile(0, "u")

                with act.Fori(0, 2) as i:
                    for c in range(12):
                        n = n0 + U_CONV + c
                        act.wait_ge(dense_ready, 12 * i + (n + 1))
                        act.wait_ge(conv_step, 28 * i + (7 * (8 * b + (c - 4) // 3 + 1) + START))
                        act.activation(stage[n % 4][:, :, :], dense_ps[n % 4][:, :, :], ACT.Copy).then_inc(dense_out, 1)
                if with_rows:
                    peer_tile(0, "v")

                with act.Fori(0, 8) as i:
                    for c in range(4):
                        n = n0 + U_GATE + c
                        act.wait_ge(dense_ready, 4 * i + (n + 1))
                        if c == 0:
                            act.wait_ge(conv_step, 56 * (b + 1) + START)
                            act.wait_ge(gate_step, 3 * i + (24 * b + START))
                        if c < 2:
                            for ct in range(2):
                                a = act.activation(stage[n % 4][:, ct, :], dense_ps[n % 4][:, ct, :], ACT.Sigmoid,
                                                   bias=vecs[:, bass.ds(2 * i + (16 * c + ct), 1)])
                            a.then_inc(dense_out, 1)
                        else:
                            act.activation(stage[n % 4][:, :, :], dense_ps[n % 4][:, :, :], ACT.Copy
                                           ).then_inc(dense_out, 1)
                if with_rows:
                    peer_tile(1, "u")

                with act.Fori(0, 2) as i:
                    for c in range(4):
                        n = n0 + U_OUT + c
                        act.wait_ge(dense_ready, 4 * i + (n + 1))
                        act.wait_ge(gate_step, 24 * (b + 1) + START)
                        act.wait_ge(out_step, 4 * i + (8 * b + c - 3 + START))
                        act.activation(stage[n % 4][:, :, :], dense_ps[n % 4][:, :, :], ACT.Copy).then_inc(dense_out, 1)
                act.wait_ge(stats_step, 10 * (b + 1))
                act.activation(sd[:, :], mv[:, :, 1], ACT.Sqrt, bias=eps[:, :]).then_inc(sd_ready, 1)
                move_transposes(2 * b + 1)

                with act.Fori(0, 2) as i:
                    for c in range(4):
                        n = n0 + U_PQ + c
                        act.wait_ge(dense_ready, 4 * i + (n + 1))
                        act.activation(stage[n % 4][:, :, :], dense_ps[n % 4][:, :, :], ACT.Copy).then_inc(dense_out, 1)
                        act.wait_ge(ks_ready, 4 * i + (8 * b + c + 1))
                        act.wait_ge(pick_step, 48 * i + ((12 * (8 * b + c - 2) + 2) + START))
                        act.activation(ks[:, c % 2, :, :, :].rearrange("p t a k -> p (t a k)"),
                                       score_ps[c % 2][:, :, :].rearrange("p t k -> p (t k)"), ACT.Copy
                                       ).then_inc(ks_out, 1)
                act.wait_ge(gather_step, 14 * b + 1)
                act.activation(gate[:, b, :, :], gate[:, b, :, :], ACT.Exp).then_inc(gexp_ready, 1)
                if with_rows:
                    peer_tile(1, "v")
                if not OVERLAP or b == 1:
                    for t in range(b * TILES, (b + 1) * TILES):
                        peer_tile(t, "uv")
            act.wait_ge(out_sent, 16 * HALVES * TILES)

        @block.tensor
        def _(pe):
            pe.wait_ge(masks_ok, 4)
            pe.wait_ge(small_in, 96)
            nc.tensor.transpose(oT_ps[:, 0:80], vecs_in, ident[0:80, 0:80]).then_inc(setup_ready, 1)
            for q in range(4):
                for g in range(4):
                    last = nc.tensor.transpose(dense_ps[q][:, :, :].rearrange("p c t -> p (c t)")[:, g * P:(g + 1) * P],
                                               subk[:, 4 * q + g, :], ident[:, :])
                last.then_inc(setup_ready, 1)

            def transposes(call, src):
                for r in range(8):
                    if 8 * call + r >= 2:
                        pe.wait_ge(tr_done, 8 * call + r - 1)
                    for k in range(2):
                        for t in range(TILES):
                            last = nc.tensor.transpose(score_ps[r % 2][:, k, t * P:(t + 1) * P],
                                                       src[:, t, (2 * r + k) * P:(2 * r + k + 1) * P], ident[:, :])
                    last.then_inc(tr_ready, 1)

            def mm_T(n, src, c, k0=0, k1=KT):
                for k in range(k0, k1):
                    last = nc.tensor.matmul(dense_ps[n % 4][:, c, :], wbuf[n % 2][:, k, c * P:(c + 1) * P],
                                            src[:, k, :], start=(k == 0), stop=(k == KT - 1))
                return last

            def begin(n, per, i):
                b = n // UNITS
                pe.wait_ge(w_ready[n % 2], (8 * per) * i + 16 * (n // 2 - b))
                if n >= 4:
                    pe.wait_ge(dense_out, per * i + (n - 3))

            def unit_T(n, src, per=0, i=0):
                begin(n, per, i)
                mm_T(n, src, 0)
                mm_T(n, src, 1).then_inc(dense_ready, 1)

            def unit_tokens(n, src, per=0, i=0):
                begin(n, per, i)
                for t in range(TILES):
                    for k in range(KT):
                        last = nc.tensor.matmul(dense_ps[n % 4][:, t, :], src[:, k, t * P:(t + 1) * P],
                                                wbuf[n % 2][:, k, :], start=(k == 0), stop=(k == KT - 1))
                last.then_inc(dense_ready, 1)

            for b in range(HALVES):
                n0 = UNITS * b
                pe.wait_ge(x_in, 16 * (b + 1))
                if b:
                    pe.wait_ge(ks_out, 8 * b + START)
                transposes(2 * b, hs[b])
                pe.wait_ge(tr_done, 16 * b + 8)
                if not b:
                    pe.wait_ge(setup_done, 5)
                for u in range(2):
                    n = n0 + U_K + u
                    pe.wait_ge(k_ready[u], 64 * (b + 1))
                    if n >= 4:
                        pe.wait_ge(dense_out, n - 3)
                    mm_T(n, xT, 0)
                    mm_T(n, xT, 1).then_inc(dense_ready, 1)
                unit_tokens(n0 + U_V, xT)
                unit_T(n0 + U_Q, xT)
                pe.wait_ge(dense_out, n0 + U_Q)

                with pe.Fori(0, 2) as i:
                    for u in range(4):
                        n = n0 + U_Q + u
                        pe.wait_ge(dense_out, 4 * i + (n + 1))
                        if u % 2 == 0:
                            pe.wait_ge(keys_ready, 2 * i + (4 * b + u // 2 + 1))
                        q = stage[n % 4]
                        for t in range(TILES):
                            s = 16 * b + 2 * u + t
                            for at, h in enumerate(ORDER):
                                lo = (h % 2) * HD
                                pe.wait_ge(pT_copied, 16 * i + (2 * s + at // 2 - 1 + START))
                                nc.tensor.matmul(score_ps[at // 2][:, at % 2, :],
                                                 q[lo:lo + HD, h // 2, t * P:(t + 1) * P],
                                                 keys[lo:lo + HD, u // 2, t * P:t * P + 2 * P],
                                                 start=True, stop=True).then_inc(scores_ready, 1)
                            if t == 0:
                                begin(n + 1, 4, i)
                            mm_T(n + 1, xT, t, 0, 12)
                            for at, h in enumerate(ORDER):
                                pe.wait_ge(exp_done, 32 * i + (4 * s + at + 1 + START))
                                for c in range(2):
                                    last = nc.tensor.transpose(score_ps[at // 2][:, at % 2, c * P:(c + 1) * P],
                                                               probs[:, h, c * P:(c + 1) * P], ident[:, :])
                                if at % 2:
                                    last.then_inc(pT_ready, 1)
                            pe.wait_ge(attn_ready, 8 * i + (s + START))
                            for at, h in enumerate(ORDER):
                                pe.wait_ge(pT_copied, 16 * i + (2 * s + at // 2 + 1 + START))
                                for c in range(2):
                                    last = nc.tensor.matmul(o_ps[:, h, :], pT[:, at, c * P:(c + 1) * P],
                                                            v[:, t + c, bass.ds(i * (2 * HD) + (u // 2) * HD, HD)],
                                                            start=(c == 0), stop=(c == 1))
                            last.then_inc(o_ready, 1)
                            last = mm_T(n + 1, xT, t, 12, KT)
                            if t == 1:
                                last.then_inc(dense_ready, 1)
                            pe.wait_ge(attn_ready, 8 * i + (s + 1 + START))
                            pe.wait_ge(aT_done, 8 * i + (s + START))
                            for c in range(2):
                                last = nc.tensor.transpose(oT_ps[:, c * P:(c + 1) * P], attn[:, c * P:(c + 1) * P],
                                                           ident[:, :])
                            last.then_inc(oT_ready, 1)

                for c in range(1, 4):
                    unit_T(n0 + U_CONV + c, xT)
                with pe.Fori(0, 5) as i:
                    for c in range(4):
                        unit_T(n0 + U_CONV + 4 + c, xT, 4, i)

                pe.wait_ge(aT_done, 16 * (b + 1) + START)
                pe.wait_ge(conv_step, 56 * (b + 1) + START)
                with pe.Fori(0, 8) as i:
                    for c, src in enumerate((xT, xT, aT, cT)):
                        unit_T(n0 + U_GATE + c, src, 4, i)

                pe.wait_ge(gate_step, 24 * (b + 1) + START)
                with pe.Fori(0, 2) as i:
                    for c in range(4):
                        unit_tokens(n0 + U_OUT + c, mT, 4, i)

                pe.wait_ge(h_ready, TILES * (b + 1))
                transposes(2 * b + 1, hs[b])
                pe.wait_ge(tr_done, 16 * b + 16)
                with pe.Fori(0, 2) as i:
                    for c in range(4):
                        n = n0 + U_PQ + c
                        unit_T(n, xT, 4, i)
                        pe.wait_ge(dense_out, 4 * i + (n + 1))
                        pe.wait_ge(ks_out, 4 * i + (8 * b + c - 1 + START))
                        for t in range(TILES):
                            for a in range(2):
                                last = nc.tensor.matmul(score_ps[c % 2][:, t, a * NK:(a + 1) * NK],
                                                        stage[n % 4][:, a, t * P:(t + 1) * P],
                                                        skT[:, bass.ds(8 * i + 2 * c + a, 1), :], start=True, stop=True)
                        last.then_inc(ks_ready, 1)

        @block.vector
        def _(dve):
            V = nc.vector

            class Rows:

                def __init__(self, on, t, part, per, i, base=0):
                    self.on, self.t, self.part, self.per, self.i, self.at = on, t, part, per, i, base

                def use(self, count):
                    if not self.on:
                        return
                    t, per, i = self.t, self.per, self.i
                    for _ in range(count):
                        slot = self.at % RING
                        g = t * ROWS + self.part * SLOTS + self.at
                        dve.wait_ge(row_in[slot], (16 * per // RING) * i + 16 * (g // RING + 1))
                        col = per * i + self.at
                        if self.part == 0:
                            V.scalar_tensor_tensor(out=row[slot][:, :], in0=row[slot][:, :], scalar=1.0,
                                                   in1=hs[t // TILES][:, t % TILES, :], op0=ALU.mult, op1=ALU.mult,
                                                   accum_out=dots[:, bass.ds(col, 1)]).then_inc(row_used, 1)
                        else:
                            dve.wait_ge(row_used, per * i + (g + START))
                            V.scalar_tensor_tensor(out=y[:, :], in0=row[slot][:, :], scalar=wgt[:, bass.ds(col, 1)],
                                                   in1=y[:, :], op0=ALU.mult, op1=ALU.add).then_inc(row_used, 1)
                        self.at += 1

            def weigh(t):
                dve.wait_ge(gelu_ready, t + 1)
                V.tensor_tensor(wgt[:, :], gelu[:, :], gate[:, t // TILES, t % TILES, :], ALU.mult).then_inc(wgt_ready, 1)
                dve.wait_ge(wgt_ready, t + 1)
                dve.wait_ge(y_init, t + 1)

            def finish_tile(t):
                f = 9 * t
                dve.wait_ge(row_used, ROWS * (t + 1) + START)
                for c in range(4):
                    V.bn_stats(bst2[:, c, :], y[:, c * 512:(c + 1) * 512]).then_inc(fin_step, 1)
                dve.wait_ge(fin_step, f + 4)
                V.bn_aggr(mv2[:, :], bst2[:, :, :].rearrange("p c s -> p (c s)")).then_inc(fin_step, 1)
                dve.wait_ge(sd2_ready, t + 1)
                V.reciprocal(rstd2[:, :], sd2[:, :]).then_inc(fin_step, 1)
                dve.wait_ge(fin_step, f + 6)
                V.tensor_scalar(y[:, :], y[:, :], mv2[:, 0:1], rstd2[:, :], ALU.subtract, ALU.mult).then_inc(fin_step, 1)
                dve.wait_ge(fin_step, f + 7)
                V.tensor_tensor(y[:, :], y[:, :], ln2[:, 0, :], ALU.mult).then_inc(fin_step, 1)
                dve.wait_ge(fin_step, f + 8)
                V.tensor_tensor(y[:, :], y[:, :], ln2[:, 1, :], ALU.add).then_inc(fin_step, 1)

            for count in (masked, exp_done, pT_copied, attn_ready, aT_done, oT_ready, conv_step, gate_step, out_step,
                          pick_step, ks_out, row_used):
                dve.sem_inc(count, START)
            V.memset(kT[:, :, 0:P], 0.0)
            V.memset(v[:, 0, :], 0.0)
            V.memset(carry[:, :, :], 0.0)
            V.memset(eps[:, :], EPS).then_inc(const_ok, 1)
            dve.wait_ge(small_in, 96)
            V.tensor_scalar(nsink[:, :], sink[:, :], -1.0, None, ALU.mult).then_inc(nsink_ok, 1)
            dve.wait_ge(nsink_ok, 1)
            dve.wait_ge(const_ok, 1)
            dve.wait_ge(masks_ok, 7)
            dve.wait_ge(setup_done, 5)

            for b in range(HALVES):
                rows_on = b == 1 and OVERLAP
                with dve.Fori(0, 2) as i:
                    rows = Rows(rows_on, 0, 0, 64, i)
                    for u in range(4):
                        for t in range(TILES):
                            s = 16 * b + 2 * u + t
                            for at, h in enumerate(ORDER):
                                dve.wait_ge(scores_ready, 32 * i + (4 * s + 2 * (at // 2) + 2))
                                dve.wait_ge(exp_done, 32 * i + (4 * s + at - 3 + START))
                                dve.sem_inc(went_on, 1)
                                V.tensor_tensor_reduce(out=sm[:, h, :], in0=score_ps[at // 2][:, at % 2, :],
                                                       in1=mask[:, 1 if b or t else 0, :], scale=-(HD ** -0.5),
                                                       scalar=3.0e38, op0=ALU.add, op1=ALU.min,
                                                       accum_out=nmax[:, h:h + 1]).then_inc(masked, 1)
                                rows.use(2)
                            dve.wait_ge(masked, 32 * i + (4 * (s + 1) + START))
                            heads = bass.ds(16 * i + 4 * u, 4)
                            V.tensor_tensor(nmx[:, :], nmax[:, :], nsink[:, heads], ALU.min).then_inc(nmax_ready, 1)
                            dve.wait_ge(nmax_ready, 8 * i + (s + 1))
                            V.tensor_tensor(sarg[:, :], nmx[:, :], sink[:, heads], ALU.add).then_inc(sarg_ready, 1)
                            dve.wait_ge(esink_ready, 8 * i + (s + 1))
                            V.tensor_tensor(den[:, :], rowsum[:, :], esink[:, :], ALU.add).then_inc(den_ready, 1)
                            dve.wait_ge(den_ready, 8 * i + (s + 1))
                            V.reciprocal(rden[:, :], den[:, :]).then_inc(rden_ready, 1)
                            dve.wait_ge(rden_ready, 8 * i + (s + 1))
                            dve.wait_ge(o_ready, 8 * i + (s + 1))
                            dve.wait_ge(oT_ready, 8 * i + (s + START))
                            V.tensor_tensor(attn.rearrange("p (h d) -> p h d", h=4),
                                            o_ps[:, :, :],
                                            rden[:, :].unsqueeze(2).to_broadcast([P, 4, HD]), ALU.mult
                                            ).then_inc(attn_ready, 1)
                if rows_on:
                    weigh(0)

                with dve.Fori(0, 2) as i:
                    rows = Rows(rows_on, 0, 1, 64, i)
                    for c in range(4):
                        n = UNITS * b + U_CONV + 3 * c
                        f = 56 * b + 7 * c
                        sB, sC, sH = stage[n % 4], stage[(n + 1) % 4], stage[(n + 2) % 4]
                        ch = bass.ds(8 * i + 2 * c, 2)
                        dve.wait_ge(conv_step, 28 * i + (f + START))
                        dve.sem_inc(went_on, 1)
                        V.tensor_copy(uconv[:, :, 0:2], carry[:, ch, :]).then_inc(conv_step, 1)
                        dve.wait_ge(dense_out, 12 * i + (n + 3))
                        V.tensor_tensor(uconv[:, :, 2:2 + HALF], sC[:, :, :], sH[:, :, :], ALU.mult
                                        ).then_inc(conv_step, 1)
                        rows.use(6)
                        dve.wait_ge(conv_step, 28 * i + (f + 2 + START))
                        dve.sem_inc(went_on, 1)
                        V.tensor_copy(carry[:, ch, :], uconv[:, :, HALF:HALF + 2]).then_inc(conv_step, 1)
                        for ct in range(2):
                            last = V.tensor_scalar(sC[:, ct, :], uconv[:, ct, 0:HALF],
                                                   vecs[:, bass.ds(8 * i + (32 + 2 * c + ct), 1)], None, ALU.mult)
                        last.then_inc(conv_step, 1)
                        for tap in (1, 2):
                            dve.wait_ge(conv_step, 28 * i + (f + 3 + tap + START))
                            for ct in range(2):
                                last = V.scalar_tensor_tensor(
                                    out=sC[:, ct, :], in0=uconv[:, ct, tap:tap + HALF],
                                    scalar=vecs[:, bass.ds(8 * i + (32 + 16 * tap + 2 * c + ct), 1)],
                                    in1=sC[:, ct, :], op0=ALU.mult, op1=ALU.add)
                            last.then_inc(conv_step, 1)
                        dve.wait_ge(conv_step, 28 * i + (f + 6 + START))
                        V.tensor_tensor(cT[:, ch, :], sC[:, :, :], sB[:, :, :], ALU.mult).then_inc(conv_step, 1)
                        rows.use(10)
                if rows_on:
                    finish_tile(0)

                with dve.Fori(0, 8) as i:
                    rows = Rows(rows_on, 1, 0, 16, i)
                    n = UNITS * b + U_GATE
                    f = 24 * b
                    g1, g2, pa, pc = (stage[(n + c) % 4] for c in range(4))
                    rows.use(4)
                    dve.wait_ge(dense_out, 4 * i + (n + 3))
                    V.tensor_tensor(g1[:, :, :], g1[:, :, :], pa[:, :, :], ALU.mult).then_inc(gate_step, 1)
                    rows.use(6)
                    dve.wait_ge(dense_out, 4 * i + (n + 4))
                    V.tensor_tensor(g2[:, :, :], g2[:, :, :], pc[:, :, :], ALU.mult).then_inc(gate_step, 1)
                    dve.wait_ge(gate_step, 3 * i + (f + 2 + START))
                    V.tensor_tensor(mT[:, bass.ds(2 * i, 2), :], g1[:, :, :], g2[:, :, :], ALU.add).then_inc(gate_step, 1)
                    rows.use(6)
                if rows_on:
                    weigh(1)

                if b:
                    dve.wait_ge(xres_in, 16)
                with dve.Fori(0, 2) as i:
                    rows = Rows(rows_on, 1, 1, 32, i)
                    for c in range(4):
                        n = UNITS * b + U_OUT + c
                        at = hs[b][:, :, bass.ds(i * (4 * UC) + c * UC, UC)]
                        dve.wait_ge(dense_out, 4 * i + (n + 1))
                        V.scalar_tensor_tensor(out=at, in0=at, scalar=ALPHA, in1=stage[n % 4][:, :, :],
                                               op0=ALU.mult, op1=ALU.add).then_inc(out_step, 1)
                        rows.use(8)
                dve.wait_ge(out_step, 8 * (b + 1) + START)
                for t in range(TILES):
                    for c in range(4):
                        V.bn_stats(bst[:, t, c, :], hs[b][:, t, c * 512:(c + 1) * 512]).then_inc(stats_step, 1)
                for t in range(TILES):
                    dve.wait_ge(stats_step, 10 * b + 8)
                    V.bn_aggr(mv[:, t, :], bst[:, t, :, :].rearrange("p c s -> p (c s)")).then_inc(stats_step, 1)
                dve.wait_ge(sd_ready, b + 1)
                V.reciprocal(rstd[:, :], sd[:, :]).then_inc(ln_step, 1)
                dve.wait_ge(ln_step, 5 * b + 1)
                dve.wait_ge(ln1_in, 32 * (b + 1))
                for t in range(TILES):
                    V.tensor_scalar(hs[b][:, t, :], hs[b][:, t, :], mv[:, t, 0:1], rstd[:, t:t + 1],
                                    ALU.subtract, ALU.mult).then_inc(ln_step, 1)
                for t in range(TILES):
                    dve.wait_ge(ln_step, 5 * b + 2 + t)
                    V.tensor_tensor(hs[b][:, t, :], hs[b][:, t, :], ln1[:, 0, :], ALU.mult).then_inc(ln_step, 1)
                for t in range(TILES):
                    dve.wait_ge(ln_step, 5 * b + 4 + t)
                    V.tensor_tensor(hs[b][:, t, :], hs[b][:, t, :], ln1[:, 1, :], ALU.add).then_inc(h_ready, 1)

                with dve.Fori(0, 2) as i:
                    rows = Rows(rows_on, 1, 1, 32, i, base=SLOTS // 2)
                    for c in range(4):
                        f = 12 * (8 * b + c)
                        sc = ks[:, c % 2, :, :, :]
                        both = [(t, a) for t in range(TILES) for a in range(2)]

                        def step(k):
                            dve.wait_ge(pick_step, 48 * i + (f + k + START))
                            dve.sem_inc(went_on, 1)

                        rows.use(8)
                        dve.wait_ge(ks_out, 4 * i + (8 * b + c + 1 + START))
                        dve.sem_inc(went_on, 1)
                        for t, a in both:
                            last = V.max(tops[:, t, a, 0:8], sc[:, t, a, :])
                        last.then_inc(pick_step, 1)
                        step(1)
                        for t, a in both:
                            V.max_index(topi[:, t, a, 0:8], tops[:, t, a, 0:8], sc[:, t, a, :])
                        for t, a in both:
                            last = V.match_replace(ksw[:, t, a, :], tops[:, t, a, 0:8], sc[:, t, a, :], LOWEST)
                        last.then_inc(pick_step, 1)
                        step(2)
                        for t, a in both:
                            last = V.max(tops[:, t, a, 8:16], ksw[:, t, a, :])
                        last.then_inc(pick_step, 1)
                        step(3)
                        for t, a in both:
                            last = V.max_index(topi[:, t, a, 8:16], tops[:, t, a, 8:16], ksw[:, t, a, :])
                        last.then_inc(pick_step, 1)
                        for t in range(TILES):
                            last = V.tensor_tensor(cand[:, t, :].rearrange("p (a b) -> p a b", a=TOPK),
                                                   tops[:, t, 0, :].unsqueeze(2).to_broadcast([P, TOPK, TOPK]),
                                                   tops[:, t, 1, :].unsqueeze(1).to_broadcast([P, TOPK, TOPK]), ALU.add)
                        last.then_inc(pick_step, 1)
                        step(5)
                        for t in range(TILES):
                            last = V.max(bests[:, t, 0:8], cand[:, t, :])
                        last.then_inc(pick_step, 1)
                        step(6)
                        for t in range(TILES):
                            V.max_index(bestp[:, t, 0:8], bests[:, t, 0:8], cand[:, t, :])
                        for t in range(TILES):
                            last = V.match_replace(candw[:, t, :], bests[:, t, 0:8], cand[:, t, :], LOWEST)
                        last.then_inc(pick_step, 1)
                        step(7)
                        for t in range(TILES):
                            last = V.max(bests[:, t, 8:16], candw[:, t, :])
                        last.then_inc(pick_step, 1)
                        step(8)
                        for t in range(TILES):
                            last = V.max_index(bestp[:, t, 8:16], bests[:, t, 8:16], candw[:, t, :])
                        last.then_inc(pick_step, 1)
                        V.tensor_copy(best[:, :, bass.ds(4 * i + c, 1), :].rearrange("p t o k -> p (t o) k"), bests
                                      ).then_inc(pick_step, 1)
                        step(9)
                        V.tensor_scalar(posab[:, :, 0, :], bestp, 4, None, ALU.logical_shift_right)
                        V.tensor_scalar(posab[:, :, 1, :], bestp, 15, None, ALU.bitwise_and).then_inc(pick_step, 1)
                        step(11)
                        fo = found[:, :, bass.ds(4 * i + c, 1), :].rearrange("p t o k -> p (t o) k")
                        V.tensor_copy(fo[:, :, 0:32], posab.rearrange("p t a k -> p t (a k)"))
                        V.tensor_copy(fo[:, :, 32:64], topi.rearrange("p t a k -> p t (a k)")).then_inc(pick_step, 1)
                        step(12)

                f = 14 * b
                V.tensor_tensor(gate[:, b, :, :].rearrange("p t (h k) -> p (t h) k", h=PH),
                                best[:, :, :, :].rearrange("p t h k -> p (t h) k"),
                                best[:, :, :, 0:1].rearrange("p t h k -> p (t h) k").to_broadcast([P, TILES * PH, TOPK]),
                                ALU.subtract).then_inc(gather_step, 1)
                k = 1
                for t in range(TILES):
                    for a, key in ((0, key0), (1, key1)):
                        pos = found[:, t, :, a * TOPK:(a + 1) * TOPK].unsqueeze(3).to_broadcast([P, PH, TOPK, TOPK])
                        num = found[:, t, :, (2 + a) * TOPK:(3 + a) * TOPK].unsqueeze(2).to_broadcast([P, PH, TOPK, TOPK])
                        if k > 1:
                            dve.wait_ge(gather_step, f + k)
                        V.tensor_tensor(onehot, pos, iota[:, :].unsqueeze(1).unsqueeze(1).to_broadcast([P, PH, TOPK, TOPK]),
                                        ALU.is_equal).then_inc(gather_step, 1)
                        k += 1
                        dve.wait_ge(gather_step, f + k)
                        V.tensor_tensor(onehot, onehot, num, ALU.mult).then_inc(gather_step, 1)
                        k += 1
                        dve.wait_ge(gather_step, f + k)
                        V.tensor_reduce(key.rearrange("p (h k) -> p h k", h=PH), onehot, AX.X, ALU.add
                                        ).then_inc(gather_step, 1)
                        k += 1
                    dve.wait_ge(gather_step, f + k)
                    V.scalar_tensor_tensor(out=expert[:, b, t, :], in0=key0, scalar=float(NK), in1=key1,
                                           op0=ALU.mult, op1=ALU.add).then_inc(expert_ready, 1)
                dve.wait_ge(gexp_ready, b + 1)
                gv = gate[:, b, :, :].rearrange("p t (h k) -> p (t h) k", h=PH)
                V.tensor_reduce(gsum[:, :, :].rearrange("p t h -> p (t h)"), gv, AX.X, ALU.add).then_inc(gather_step, 1)
                dve.wait_ge(gather_step, f + 14)
                V.reciprocal(grec[:, :, :], gsum[:, :, :]).then_inc(gate_norm, 1)
                dve.wait_ge(gate_norm, 2 * b + 1)
                V.tensor_tensor(gv, gv, grec[:, :, :].rearrange("p t h -> p (t h)").unsqueeze(2)
                                .to_broadcast([P, TILES * PH, TOPK]), ALU.mult).then_inc(gate_norm, 1)
                dve.wait_ge(gate_norm, 2 * b + 2)
                if rows_on:
                    finish_tile(1)
                if not OVERLAP or b == 1:
                    for t in range(b * TILES, (b + 1) * TILES):
                        for part in range(2):
                            if part:
                                weigh(t)
                            with dve.Fori(0, 8) as i:
                                Rows(True, t, part, 16, i).use(16)
                        finish_tile(t)


_OUTS = [((1, SEQ, D), 'float32')]
_INS = ["x", "w_in", "b_gate", "sinks", "conv_w", "w_attn_out", "w_conv_out", "w_o", "ln1_g", "ln1_b",
        "peer_w_q", "peer_sub_keys", "peer_u", "peer_v", "ln2_g", "ln2_b"]


def kernel(**inputs):
    import numpy as _np
    import concourse.bacc as _bacc
    from concourse import mybir as _mybir
    from concourse.bass_utils import run_bass_kernel_spmd as _run

    nc = _bacc.Bacc("TRN2", target_bir_lowering=False, num_devices=1)
    arrays, args = {}, []
    for name in _INS:
        a = _np.ascontiguousarray(inputs[name])
        arrays[f"in_{name}_dram"] = a
        args.append(nc.dram_tensor(f"in_{name}_dram", a.shape, _mybir.dt.from_np(a.dtype), kind="ExternalInput").ap())
    for i, (shape, dtype) in enumerate(_OUTS):
        dt = _mybir.dt.from_np(_np.dtype(dtype))
        args.append(nc.dram_tensor(f"out_{i}_dram", shape, dt, kind="ExternalOutput").ap())
    build(nc, *args)
    r = _run(nc, [arrays], core_ids=[0])
    return r.results[0]["out_0_dram"]
```

```python
import concourse.bass as bass
from concourse import mybir
from contextlib import ExitStack

F32 = mybir.dt.float32
F32R = mybir.dt.float32r
U32 = mybir.dt.uint32
ALU = mybir.AluOpType
ACT = mybir.ActivationFunctionType
AX = mybir.AxisListType

P = 128
D = 2048
SEQ = 512
HALF = 256
TILES = HALF // P
HALVES = SEQ // HALF
KT = D // P
HD = 64
HEADS = 32
KV_HEADS = 4
EPS = 1e-5
ALPHA = 2.0 ** 0.25
NEG = -1e30
LOWEST = -3.4e38

UC = 256
K_OFF = HEADS * HD
V_OFF = K_OFF + KV_HEADS * HD
CB_OFF = V_OFF + KV_HEADS * HD
CC_OFF = CB_OFF + D
CH_OFF = CC_OFF + D
G_OFF = CH_OFF + D

ORDER = (0, 2, 1, 3)
U_K = 0
U_V = 2
U_Q = 3
U_GA = 11
U_CONV = 27
U_GC = 51
U_OUT = 67
U_PQ = 75
UNITS = 83

PH = 8
NK = 128
TOPK = 16
SLOTS = PH * TOPK
ROWS = 2 * SLOTS
RING = 4
OVERLAP = True
START = 32


def build(nc, x, w_in, b_gate, sinks, conv_w, w_attn_out, w_conv_out, w_o, ln1_g, ln1_b,
          peer_w_q, peer_sub_keys, peer_u, peer_v, ln2_g, ln2_b, out):
    ctx = ExitStack()
    with ctx:
        def sb(name, shape, dt=F32):
            return ctx.enter_context(nc.sbuf_tensor(name, shape, dt))

        def over(tensor_at, name, shape):
            return nc.alloc_sbuf_tensor_at(name, shape, F32R, offset=tensor_at)

        def at(name, shape):
            t = sb(name, shape)
            return t, nc.sbuf_base - 4 * shape[1] * (shape[2] if len(shape) > 2 else 1)

        def sem(name):
            return ctx.enter_context(nc.semaphore(name))

        wbuf = [sb(f"wbuf{i}", [P, KT, UC]) for i in range(2)]
        xT, xT_at = at("xT", [P, KT, HALF])
        aT, aT_at = at("aT", [P, KT, HALF])
        cT, cT_at = at("cT", [P, KT, HALF])
        mT = sb("mT", [P, KT, HALF])
        h0 = sb("h0", [P, TILES, D])
        row, row_at = zip(*(at(f"row{i}", [P, D]) for i in range(RING)))
        y = sb("y", [P, D])
        ln2, ln2_at = at("ln2", [P, 2, D])
        kT = sb("kT", [P, KV_HEADS, P + HALF])
        v = sb("v", [P, 1 + TILES, KV_HEADS * HD])
        stage = [sb(f"stage{i}", [P, 2, HALF]) for i in range(4)]
        uconv = sb("uconv", [P, 2, 2 + HALF])
        carry = sb("carry", [P, KT, 2])
        skT = sb("skT", [P, 2 * PH, NK])
        mask = sb("mask", [P, 2, 2 * P])
        ident = sb("ident", [P, P])
        vecs = sb("vecs", [P, 80])
        sink = sb("sink", [P, HEADS])
        nsink = sb("nsink", [P, HEADS])
        eps = sb("eps", [P, 1])
        iota = sb("iota", [P, TOPK])
        nmax = sb("nmax", [P, 4])
        nmx = sb("nmx", [P, 4])
        sarg = sb("sarg", [P, 4])
        esink = sb("esink", [P, 4])
        rowsum = sb("rowsum", [P, 4])
        den = sb("den", [P, 4])
        rden = sb("rden", [P, 4])
        bst = sb("bst", [P, TILES, 4, 6])
        mv = sb("mv", [P, TILES, 2])
        sd = sb("sd", [P, TILES])
        rstd = sb("rstd", [P, TILES])
        bst2 = sb("bst2", [P, 4, 6])
        mv2 = sb("mv2", [P, 2])
        sd2 = sb("sd2", [P, 1])
        rstd2 = sb("rstd2", [P, 1])
        gmax = sb("gmax", [P, TILES, PH])
        gsum = sb("gsum", [P, TILES, PH])
        grec = sb("grec", [P, TILES, PH])
        expert = sb("expert", [P, HALVES, TILES, SLOTS], U32)
        gate = sb("gate", [P, HALVES, TILES, SLOTS])
        cols = sb("cols", [P, 2, 16], U32)
        dots = sb("dots", [P, SLOTS])
        gelu = sb("gelu", [P, SLOTS])
        wgt = sb("wgt", [P, SLOTS])

        act_hi = over(xT_at, "act_hi", [P, KT, HALF])
        act_lo = over(ln2_at, "act_lo", [P, KT, HALF])
        br_hi = over(aT_at, "br_hi", [P, KT, HALF])
        br_lo = over(cT_at, "br_lo", [P, KT, HALF])
        w_hi = [over(row_at[c], f"w_hi{c}", [P, KT, P]) for c in range(2)]
        w_lo = [over(row_at[2 + c], f"w_lo{c}", [P, KT, P]) for c in range(2)]

        def by_k(n):
            return n == U_V or U_OUT <= n < U_PQ

        def unit_half(n, c):
            if by_k(n):
                return wbuf[n % 2][:, c * KT // 2:(c + 1) * KT // 2, :]
            return wbuf[n % 2][:, :, c * P:(c + 1) * P]

        def part_of(n, w):
            return w[:, :, :].rearrange("p (k a) q -> p k (a q)", a=2) if by_k(n) else w[:, :, :]

        mflat = mT[:, :, :].rearrange("p k t -> p (k t)")

        def scratch(at, n):
            return mflat[:, at:at + n]

        sm = scratch(0, 1024).rearrange("p (h k) -> p h k", h=4)
        probs = scratch(1024, 1024).rearrange("p (h k) -> p h k", h=4)
        pT = scratch(2048, 1024).rearrange("p (h k) -> p h k", h=4)
        attn = scratch(3072, 256)
        keys = scratch(3328, 768).rearrange("p (n k) -> p n k", n=2)
        ks = scratch(0, 1024).rearrange("p (n t a k) -> p n t a k", n=2, t=2, a=2)
        ksw = scratch(1024, 512).rearrange("p (t a k) -> p t a k", t=2, a=2)
        cand = scratch(1536, 512).rearrange("p (t k) -> p t k", t=2)
        candw = scratch(2048, 512).rearrange("p (t k) -> p t k", t=2)
        tops = scratch(2560, 64).rearrange("p (t a k) -> p t a k", t=2, a=2)
        topi = scratch(2624, 64).bitcast(U32).rearrange("p (t a k) -> p t a k", t=2, a=2)
        bests = scratch(2688, 32).rearrange("p (t k) -> p t k", t=2)
        bestp = scratch(2720, 32).bitcast(U32).rearrange("p (t k) -> p t k", t=2)
        posab = scratch(2752, 64).bitcast(U32).rearrange("p (t a k) -> p t a k", t=2, a=2)
        onehot = scratch(0, 2048).rearrange("p (h s a) -> p h s a", h=PH, s=TOPK)
        best = scratch(3840, 256).rearrange("p (t h k) -> p t h k", t=TILES, h=PH)
        found = scratch(2816, 1024).rearrange("p (t h k) -> p t h k", t=TILES, h=PH)
        key0 = scratch(2048, SLOTS)
        key1 = scratch(2176, SLOTS)
        vecs_in = mflat[0:80, 3072:3072 + P]
        subk = mflat[:, 0:2048].rearrange("p (g c) -> p g c", g=2 * PH)
        ln1 = aT[:, :, :].rearrange("p k t -> p (k t)").rearrange("p (a d) -> p a d", a=2)
        h1 = cT[:, :, :].rearrange("p k t -> p (k t)").rearrange("p (t d) -> p t d", t=TILES)
        hs = [h0[:, :, :], h1]

        dense_ps = [ctx.enter_context(nc.psum_tensor(f"dense_ps{i}", [P, 2, HALF], F32)) for i in range(4)]
        score_ps = [ctx.enter_context(nc.psum_tensor(f"score_ps{i}", [P, 2, 2 * P], F32)) for i in range(2)]
        oT_ps = ctx.enter_context(nc.psum_tensor("oT_ps", [P, 2 * P], F32))
        o_ps = ctx.enter_context(nc.psum_tensor("o_ps", [P, 4, HD], F32))

        w_ready = [sem(f"w_ready{i}") for i in range(2)]
        k_ready = [sem(f"k_ready{u}") for u in range(2)]
        w_hi_ready = sem("w_hi_ready")
        w_lo_ready = sem("w_lo_ready")
        half_used = sem("half_used")
        tr_lo = sem("tr_lo")
        m_hi = sem("m_hi")
        m_lo = sem("m_lo")
        br_split = sem("br_split")
        ln2_in = sem("ln2_in")
        small_in = sem("small_in")
        x_in = sem("x_in")
        xres_in = sem("xres_in")
        ln1_in = sem("ln1_in")
        masks_ok = sem("masks_ok")
        const_ok = sem("const_ok")
        nsink_ok = sem("nsink_ok")
        setup_ready = sem("setup_ready")
        setup_done = sem("setup_done")
        tr_ready = sem("tr_ready")
        tr_done = sem("tr_done")
        dense_ready = sem("dense_ready")
        dense_out = sem("dense_out")
        kv_shift = sem("kv_shift")
        keys_ready = sem("keys_ready")
        scores_ready = sem("scores_ready")
        masked = sem("masked")
        nmax_ready = sem("nmax_ready")
        sarg_ready = sem("sarg_ready")
        exp_done = sem("exp_done")
        esink_ready = sem("esink_ready")
        den_ready = sem("den_ready")
        rden_ready = sem("rden_ready")
        pT_ready = sem("pT_ready")
        pT_copied = sem("pT_copied")
        o_ready = sem("o_ready")
        attn_ready = sem("attn_ready")
        oT_ready = sem("oT_ready")
        aT_done = sem("aT_done")
        conv_step = sem("conv_step")
        gate_step = sem("gate_step")
        out_step = sem("out_step")
        stats_step = sem("stats_step")
        sd_ready = sem("sd_ready")
        ln_step = sem("ln_step")
        h_ready = sem("h_ready")
        ks_ready = sem("ks_ready")
        ks_out = sem("ks_out")
        pick_step = sem("pick_step")
        gather_step = sem("gather_step")
        gexp_ready = sem("gexp_ready")
        gate_norm = sem("gate_norm")
        expert_ready = sem("expert_ready")
        cols_ready = sem("cols_ready")
        row_in = [sem(f"row_in{i}") for i in range(RING)]
        row_used = sem("row_used")
        gelu_ready = sem("gelu_ready")
        y_init = sem("y_init")
        wgt_ready = sem("wgt_ready")
        fin_step = sem("fin_step")
        sd2_ready = sem("sd2_ready")
        out_sent = sem("out_sent")

        went_on = sem("went_on")
        CONV_STEPS = (9, 7)
        conv0 = (0, 8 * 9, 8 * 9 + 8 * 7)

        block = ctx.enter_context(nc.Block())

        w_in_v = w_in.rearrange("l (k p) n -> p (l k) n", p=P)
        wa_v = w_attn_out.rearrange("l (k p) n -> p (l k) n", p=P)
        wc_v = w_conv_out.rearrange("l (k p) n -> p (l k) n", p=P)
        wo_v = w_o.rearrange("l (k p) n -> p (l k) n", p=P)
        wq_v = peer_w_q.rearrange("l (k p) n -> p (l k) n", p=P)
        x_v = x.rearrange("b (t p) d -> p (b t) d", p=P)
        out_v = out.rearrange("b (t p) d -> p (b t) d", p=P)
        u_tab = peer_u.rearrange("l e d -> (l e) d")
        v_tab = peer_v.rearrange("l e d -> (l e) d")

        @block.sync
        def _(sp):
            sp.dma_start(h0[:, :, :], x_v[:, 0:TILES, :]).then_inc(x_in, 16)
            sp.dma_start(vecs_in[0:32, :], b_gate.rearrange("l (c p) -> (l c) p", p=P)).then_inc(small_in, 16)
            sp.dma_start(vecs_in[32:80, :], conv_w.rearrange("l w (c p) -> (l w c) p", p=P)).then_inc(small_in, 16)
            sp.dma_start(sink[:, :], sinks[0, :].partition_broadcast(P)).then_inc(small_in, 16)
            sp.dma_start(subk, peer_sub_keys.rearrange("l h a n c -> n (l h a) c")).then_inc(small_in, 16)

            def load(n, slot, src, col, b):
                if b:
                    sp.wait_ge(dense_ready, n - 1)
                else:
                    sp.wait_ge(w_lo_ready, n * 2 - 2)
                sp.sem_inc(went_on, 1)
                sp.dma_start(wbuf[slot][:, :, :], src[:, :, bass.ds(col, UC)]).then_inc(w_ready[slot], 16)

            for b in range(HALVES):
                n0 = UNITS * b
                if b:
                    sp.wait_ge(dense_ready, U_OUT)
                    sp.dma_start(h1, x_v[:, TILES:2 * TILES, :]).then_inc(x_in, 16)
                    sp.wait_ge(dense_ready, UNITS)
                    sp.dma_start(ln2[:, 0, :], ln2_g[0, :].partition_broadcast(P)).then_inc(ln2_in, 16)
                    sp.dma_start(ln2[:, 1, :], ln2_b[0, :].partition_broadcast(P)).then_inc(ln2_in, 16)
                for u in range(2):
                    n = n0 + U_K + u
                    if n >= 2:
                        sp.wait_ge(dense_ready, n - 1)
                    for c in range(2):
                        for twice in range(2):
                            col = K_OFF + (2 * u + c) * HD
                            sp.dma_start(wbuf[n % 2][:, :, c * P + twice * HD:c * P + (twice + 1) * HD],
                                         w_in_v[:, :, col:col + HD]).then_inc(k_ready[u], 16)
                load(n0 + U_V, (n0 + U_V) % 2, w_in_v, V_OFF, b)
                with sp.Fori(0, 4) as i:
                    for c in range(2):
                        n = n0 + U_Q + c
                        load(n + 2 * i, n % 2, w_in_v, i * (2 * UC) + c * UC, b)
                with sp.Fori(0, 8) as i:
                    for c, (src, col) in enumerate(((w_in_v, G_OFF), (wa_v, 0))):
                        n = n0 + U_GA + c
                        load(n + 2 * i, n % 2, src, i * UC + col, b)
                with sp.Fori(0, 4) as i:
                    for c in range(6):
                        n = n0 + U_CONV + c
                        load(n + 6 * i, n % 2, w_in_v, i * (2 * UC) + (CB_OFF + (c % 3) * D + (c // 3) * UC), b)
                with sp.Fori(0, 8) as i:
                    for c, (src, col) in enumerate(((w_in_v, G_OFF + D), (wc_v, 0))):
                        n = n0 + U_GC + c
                        load(n + 2 * i, n % 2, src, i * UC + col, b)
                if b:
                    sp.wait_ge(dense_ready, n0 + U_OUT)
                    sp.dma_start(h1, x_v[:, TILES:2 * TILES, :]).then_inc(xres_in, 16)
                for base, src in ((U_OUT, wo_v), (U_PQ, wq_v)):
                    with sp.Fori(0, 4) as i:
                        for c in range(2):
                            n = n0 + base + c
                            load(n + 2 * i, n % 2, src, i * (2 * UC) + c * UC, b)
                    if base == U_OUT:
                        sp.wait_ge(dense_ready, n0 + U_OUT)
                        sp.dma_start(ln1[:, 0, :], ln1_g[0, :].partition_broadcast(P)).then_inc(ln1_in, 16)
                        sp.dma_start(ln1[:, 1, :], ln1_b[0, :].partition_broadcast(P)).then_inc(ln1_in, 16)

        @block.gpsimd
        def _(pool):
            pool.memset(ident[:, :], 0.0).then_inc(masks_ok, 1)
            pool.memset(mask[:, :, :], 0.0).then_inc(masks_ok, 1)
            pool.iota(iota[:, :], [[1, TOPK]], base=0, channel_multiplier=0,
                      allow_small_or_imprecise_dtypes=True).then_inc(masks_ok, 1)
            pool.wait_ge(masks_ok, 3)
            pool.affine_select(out=ident[:, :], in_=ident[:, :], compare_op=ALU.not_equal, fill=1.0,
                               base=0, pattern=[[-1, P]], channel_multiplier=1).then_inc(masks_ok, 1)
            pool.affine_select(out=mask[:, :, :], in_=mask[:, :, :], compare_op=ALU.is_gt, fill=NEG,
                               base=0, pattern=[[0, 2], [1, 2 * P]], channel_multiplier=-1).then_inc(masks_ok, 1)
            pool.wait_ge(masks_ok, 5)
            pool.affine_select(out=mask[:, :, :], in_=mask[:, :, :], compare_op=ALU.is_ge, fill=NEG,
                               base=P, pattern=[[0, 2], [-1, 2 * P]], channel_multiplier=1).then_inc(masks_ok, 1)
            pool.wait_ge(masks_ok, 6)
            pool.memset(mask[:, 0, 0:P], NEG).then_inc(masks_ok, 1)

            for q in range(2 * U_PQ + 3, 2 * UNITS):
                n, c = q // 2, q % 2
                pool.wait_ge(w_hi_ready, q + 1)
                pool.wait_ge(w_lo_ready, q)
                nc.gpsimd.tensor_tensor(w_lo[c][:, :, :], unit_half(n, c), w_hi[c][:, :, :].bitcast(F32), ALU.subtract
                                        ).then_inc(w_lo_ready, 1)

            for t in range(HALVES * TILES):
                b = t // TILES
                pool.wait_ge(expert_ready, t + 1)
                for part, tab in ((0, u_tab), (1, v_tab)):
                    row0 = t * ROWS + part * SLOTS
                    with pool.Fori(0, 4) as i:
                        for c in range(2):
                            pool.wait_ge(row_used, 32 * i + (row0 - 16 + 16 * c + START))
                            nc.gpsimd.tensor_copy(cols[:, c, :], expert[:, b, t % TILES, bass.ds(i * 32 + 16 * c, 16)]
                                                  ).then_inc(cols_ready, 1)
                            pool.wait_ge(cols_ready, 2 * i + (row0 // 16 + c + 1))
                            for j in range(16):
                                g = row0 + 16 * c + j
                                pool.wait_ge(row_used, 32 * i + (g - RING + 1 + START))
                                pool.sem_inc(went_on, 1)
                                pool.indirect_dma_start(
                                    out=row[j % RING][:, :], out_offset=None, in_=tab[:, :],
                                    in_offset=bass.IndirectOffsetOnAxis(ap=cols[:, c, j:j + 1], axis=0),
                                ).then_inc(row_in[j % RING], 16)

        @block.scalar
        def _(act):
            def move_setup():
                act.wait_ge(setup_ready, 1)
                act.activation(vecs[:, :], oT_ps[:, 0:80], ACT.Copy).then_inc(setup_done, 1)
                for q in range(4):
                    act.wait_ge(setup_ready, 2 + q)
                    act.activation(skT[:, 4 * q:4 * q + 4, :].rearrange("p g n -> p (g n)"),
                                   dense_ps[q][:, :, :].rearrange("p c t -> p (c t)"), ACT.Copy).then_inc(setup_done, 1)

            def move_transposes(call):
                for r in range(8):
                    act.wait_ge(tr_ready, 8 * call + r + 1)
                    act.activation((xT if call > 1 else act_hi)[:, 2 * r:2 * r + 2, :].rearrange("p k t -> p (k t)"),
                                   score_ps[r % 2][:, :, :].rearrange("p k t -> p (k t)"), ACT.Copy).then_inc(tr_done, 1)

            def split_hi(n, c, per=0, i=0):
                if n >= UNITS:
                    return
                if n < 2:
                    act.wait_ge(k_ready[n], 64)
                elif c == 0:
                    act.wait_ge(w_ready[n % 2], (8 * per) * i + 16 * (n // 2))
                if n and c == 0:
                    act.wait_ge(half_used, per * i + n)
                if n and c == 1:
                    act.wait_ge(dense_ready, per * i + n)
                act.activation(part_of(n, w_hi[c]), unit_half(n, c), ACT.Copy).then_inc(w_hi_ready, 1)

            def peer_tile(t, stage_of):
                if "u" in stage_of:
                    act.wait_ge(row_used, ROWS * t + SLOTS + START)
                    act.activation(gelu[:, :], dots[:, :], ACT.Gelu).then_inc(gelu_ready, 1)
                    if t:
                        act.wait_ge(out_sent, 16 * t)
                    act.activation(y[:, :], hs[t // TILES][:, t % TILES, :], ACT.Copy, scale=ALPHA).then_inc(y_init, 1)
                if "v" in stage_of:
                    act.wait_ge(fin_step, 8 * t + 5)
                    act.activation(sd2[:, :], mv2[:, 1:2], ACT.Sqrt, bias=eps[:, :]).then_inc(sd2_ready, 1)
                    act.wait_ge(fin_step, 8 * (t + 1))
                    act.dma_start(out_v[:, t, :], y[:, :]).then_inc(out_sent, 16)

            move_setup()
            for b in range(HALVES):
                n0 = UNITS * b
                with_rows = b == 1 and OVERLAP
                move_transposes(2 * b)
                first = b == 0
                if first:
                    split_hi(0, 0)
                    split_hi(0, 1)
                if b:
                    act.wait_ge(dense_ready, n0 + 1)
                    act.activation(kT[:, :, 0:P], kT[:, :, HALF:HALF + P], ACT.Copy).then_inc(kv_shift, 1)
                    act.activation(v[:, 0, :], v[:, TILES, :], ACT.Copy).then_inc(kv_shift, 1)
                    act.wait_ge(kv_shift, 2)
                else:
                    act.wait_ge(const_ok, 1)
                for u in range(2):
                    n = n0 + U_K + u
                    if first:
                        split_hi(n + 1, 0)
                    act.wait_ge(dense_ready, n + 1)
                    act.activation(kT[:, 2 * u:2 * u + 2, P:P + HALF], dense_ps[n % 4][:, :, :], ACT.Copy
                                   ).then_inc(dense_out, 1)
                    if first:
                        split_hi(n + 1, 1)
                n = n0 + U_V
                if first:
                    split_hi(n + 1, 0)
                act.wait_ge(dense_ready, n + 1)
                act.activation(v[:, 1:1 + TILES, :], dense_ps[n % 4][:, :, :], ACT.Copy).then_inc(dense_out, 1)
                if first:
                    split_hi(n + 1, 1)
                    split_hi(n + 2, 0)

                act.wait_ge(dense_out, n + 1)
                if not b:
                    act.wait_ge(setup_done, 5)

                if b:
                    act.wait_ge(expert_ready, TILES * b)

                s0 = 16 * b
                with act.Fori(0, 2) as i:
                    for u in range(4):
                        n = n0 + U_Q + u
                        if u % 2 == 0:
                            act.activation(keys[:, u // 2, :],
                                           kT[:, bass.ds(2 * i + u // 2, 1), :].rearrange("p o k -> p (o k)"),
                                           ACT.Copy).then_inc(keys_ready, 1)
                        act.wait_ge(dense_ready, 4 * i + (n + 1))
                        act.activation(stage[n % 4][:, :, :], dense_ps[n % 4][:, :, :], ACT.Copy).then_inc(dense_out, 1)
                        for t in range(TILES):
                            s = s0 + 2 * u + t
                            act.wait_ge(nmax_ready, 8 * i + (s + 1))
                            for h in ORDER:
                                act.activation(probs[:, h, :], sm[:, h, :], ACT.Exp, bias=nmx[:, h:h + 1], scale=-1.0,
                                               accum_out=rowsum[:, h:h + 1]).then_inc(exp_done, 1)
                            act.wait_ge(sarg_ready, 8 * i + (s + 1))
                            act.activation(esink[:, :], sarg[:, :], ACT.Exp).then_inc(esink_ready, 1)
                            if first:
                                split_hi(n + 1 + t, 1 - t, 4, i)
                            for a in range(2):
                                act.wait_ge(pT_ready, 16 * i + (2 * s + a + 1))
                                act.activation(pT[:, 2 * a:2 * a + 2, :], score_ps[a][:, :, :], ACT.Copy
                                               ).then_inc(pT_copied, 1)
                            act.wait_ge(oT_ready, 8 * i + (s + 1 + START))
                            act.activation((br_hi if first else aT)[:, bass.ds(8 * i + 2 * u, 2), t * P:(t + 1) * P],
                                           oT_ps[:, :].rearrange("p (c t) -> p c t", c=2), ACT.Copy).then_inc(aT_done, 1)
                if with_rows:
                    peer_tile(0, "u")

                def split_m_hi(r):
                    act.activation(act_hi[:, 2 * r:2 * r + 2, :], mT[:, 2 * r:2 * r + 2, :], ACT.Copy).then_inc(m_hi, 1)

                def gate_units(base, group, bias, i, ahead=True):
                    for c in range(4):
                        n = n0 + base + c
                        act.wait_ge(dense_ready, 4 * i + (n + 1))
                        act.wait_ge(gate_step, group(c // 2, i))
                        if c % 2 == 0:
                            for ct in range(2):
                                last = act.activation(stage[n % 4][:, ct, :], dense_ps[n % 4][:, ct, :], ACT.Sigmoid,
                                                      bias=vecs[:, bass.ds(4 * i + (bias + c + ct), 1)])
                            last.then_inc(dense_out, 1)
                        else:
                            act.activation(stage[n % 4][:, :, :], dense_ps[n % 4][:, :, :], ACT.Copy
                                           ).then_inc(dense_out, 1)
                        if first:
                            split_hi(n + 1, 1, 4, i)
                            if c == 2 and not ahead:
                                act.wait_ge(gate_step, 24 * b + 22 + START)
                                for r in range(7):
                                    split_m_hi(r)
                            if c < 3 or ahead:
                                split_hi(n + 2, 0, 4, i)

                with act.Fori(0, 4) as i:
                    gate_units(U_GA, lambda g, i: 2 * i + (24 * b + g - 1 + START), 0, i)

                act.wait_ge(gate_step, 24 * b + 8 + START)
                with act.Fori(0, 2) as i:
                    for c in range(12):
                        n = n0 + U_CONV + c
                        act.wait_ge(dense_ready, 12 * i + (n + 1))
                        act.wait_ge(conv_step, 4 * CONV_STEPS[b] * i + (conv0[b] + CONV_STEPS[b] * ((c - 4) // 3 + 1) + START))
                        act.activation(stage[n % 4][:, :, :], dense_ps[n % 4][:, :, :], ACT.Copy).then_inc(dense_out, 1)
                        if first:
                            split_hi(n + 1, 1, 12, i)
                            split_hi(n + 2, 0, 12, i)
                if with_rows:
                    peer_tile(0, "v")

                act.wait_ge(conv_step, conv0[b + 1] + START)
                gc_free = lambda g, i: 4 * i + (24 * b + 8 + 2 * (g - 1) + START)
                with act.Fori(0, 3) as i:
                    gate_units(U_GC, gc_free, 16, i)
                gate_units(U_GC + 12, lambda g, i: gc_free(g, 3), 16 + 12, 0, ahead=False)
                if with_rows:
                    peer_tile(1, "u")
                act.wait_ge(gate_step, 24 * (b + 1) + START)
                if first:
                    split_m_hi(7)
                    split_hi(U_OUT + 1, 0)

                for part in range(2):
                    for c in range(4):
                        n = n0 + U_OUT + 4 * part + c
                        act.wait_ge(dense_ready, n + 1)
                        act.wait_ge(out_step, 8 * b + 4 * part + c - 3 + START)
                        act.activation(stage[n % 4][:, :, :], dense_ps[n % 4][:, :, :], ACT.Copy).then_inc(dense_out, 1)
                        if first:
                            split_hi(n + 1, 1)
                            if 4 * part + c < 7:
                                split_hi(n + 2, 0)
                act.wait_ge(stats_step, 10 * (b + 1))
                act.activation(sd[:, :], mv[:, :, 1], ACT.Sqrt, bias=eps[:, :]).then_inc(sd_ready, 1)
                move_transposes(2 * b + 1)
                if first:
                    split_hi(U_PQ + 1, 0)

                def query_units(i, part=0):
                    for c in range(4):
                        n = n0 + U_PQ + 4 * part + c
                        act.wait_ge(dense_ready, 4 * i + (n + 1))
                        act.activation(stage[n % 4][:, :, :], dense_ps[n % 4][:, :, :], ACT.Copy).then_inc(dense_out, 1)
                        if first:
                            split_hi(n + 1, 1, 4, i)
                        at_ = 8 * b + 4 * part + c
                        act.wait_ge(ks_ready, 4 * i + (at_ + 1))
                        act.wait_ge(pick_step, 48 * i + (12 * (at_ - 2) + 2 + START))
                        act.activation(ks[:, c % 2, :, :, :].rearrange("p t a k -> p (t a k)"),
                                       score_ps[c % 2][:, :, :].rearrange("p t k -> p (t k)"), ACT.Copy
                                       ).then_inc(ks_out, 1)
                        if first:
                            split_hi(n + 2, 0, 4, i)

                if first:
                    query_units(0)
                    query_units(0, 1)
                else:
                    with act.Fori(0, 2) as i:
                        query_units(i)
                act.wait_ge(gather_step, 14 * b + 1)
                act.activation(gate[:, b, :, :], gate[:, b, :, :], ACT.Exp).then_inc(gexp_ready, 1)
                if with_rows:
                    peer_tile(1, "v")
                if not OVERLAP or b == 1:
                    for t in range(b * TILES, (b + 1) * TILES):
                        peer_tile(t, "uv")
            act.wait_ge(out_sent, 16 * HALVES * TILES)

        @block.tensor
        def _(pe):
            pe.wait_ge(masks_ok, 4)
            pe.wait_ge(small_in, 64)
            nc.tensor.transpose(oT_ps[:, 0:80], vecs_in, ident[0:80, 0:80]).then_inc(setup_ready, 1)
            for q in range(4):
                for g in range(4):
                    last = nc.tensor.transpose(dense_ps[q][:, :, :].rearrange("p c t -> p (c t)")[:, g * P:(g + 1) * P],
                                               subk[:, 4 * q + g, :], ident[:, :])
                last.then_inc(setup_ready, 1)

            def transposes(call, src):
                for r in range(8):
                    if 8 * call + r >= 2:
                        if call < 2 or (call == 2 and r < 2):
                            pe.wait_ge(tr_lo, 8 * call + r - 1)
                        else:
                            pe.wait_ge(tr_done, 8 * call + r - 1)
                    if call % 2 and r % 4 == 0:
                        pe.wait_ge(h_ready, TILES * (call + r // 4))
                    for k in range(2):
                        for t in range(TILES):
                            last = nc.tensor.transpose(score_ps[r % 2][:, k, t * P:(t + 1) * P],
                                                       src[:, t, (2 * r + k) * P:(2 * r + k + 1) * P], ident[:, :])
                    last.then_inc(tr_ready, 1)

            def mm_T(n, src, c, k0=0, k1=KT):
                for k in range(k0, k1):
                    last = nc.tensor.matmul(dense_ps[n % 4][:, c, :], wbuf[n % 2][:, k, c * P:(c + 1) * P],
                                            src[:, k, :], start=(k == 0), stop=(k == KT - 1))
                return last

            def begin(n, per, i):
                if n >= UNITS:
                    pe.wait_ge(w_ready[n % 2], (8 * per) * i + 16 * (n // 2 - 1))
                if n >= 4:
                    pe.wait_ge(dense_out, per * i + (n - 3))

            def passes(out, w, x, k, opens=True, closes=True):
                first, last = opens and k == 0, closes and k == KT - 1
                nc.tensor.matmul(out, w[0](k), x[0](k), start=first, stop=False)
                nc.tensor.matmul(out, w[0](k), x[1](k), start=False, stop=False)
                return nc.tensor.matmul(out, w[1](k), x[0](k), start=False, stop=last)

            def half_T(n, src, c, per=0, i=0, k0=0, k1=KT):
                if n < UNITS and k0 == 0:
                    pe.wait_ge(w_lo_ready, (2 * per) * i + (2 * n + c + 1))
                for k in range(k0, k1):
                    if n < UNITS:
                        last = passes(dense_ps[n % 4][:, c, :],
                                      [lambda k: w_hi[c][:, k, :], lambda k: w_lo[c][:, k, :]],
                                      [lambda k: src[0][:, k, :], lambda k: src[1][:, k, :]], k)
                    else:
                        last = nc.tensor.matmul(dense_ps[n % 4][:, c, :], wbuf[n % 2][:, k, c * P:(c + 1) * P],
                                                src[:, k, :], start=(k == 0), stop=(k == KT - 1))
                if k1 == KT:
                    if c:
                        last.then_inc(dense_ready, 1)
                    elif n < UNITS:
                        last.then_inc(half_used, 1)

            def unit_T(n, src, per=0, i=0):
                begin(n, per, i)
                half_T(n, src, 0, per, i)
                half_T(n, src, 1, per, i)

            def unit_tokens(n, src, per=0, i=0):
                begin(n, per, i)
                if n < UNITS:
                    for c in range(2):
                        pe.wait_ge(w_lo_ready, (2 * per) * i + (2 * n + c + 1))
                        for t in range(TILES):
                            tok = slice(t * P, (t + 1) * P)
                            for k in range(c * KT // 2, (c + 1) * KT // 2):
                                last = passes(dense_ps[n % 4][:, t, :],
                                              [lambda k: src[0][:, k, tok], lambda k: src[1][:, k, tok]],
                                              [lambda k: part_of(n, w_hi[c])[:, k - c * KT // 2, :],
                                               lambda k: part_of(n, w_lo[c])[:, k - c * KT // 2, :]], k,
                                              opens=t == 0, closes=t == TILES - 1)
                        last.then_inc(dense_ready if c else half_used, 1)
                    return
                for t in range(TILES):
                    for k in range(KT):
                        last = nc.tensor.matmul(dense_ps[n % 4][:, t, :], src[:, k, t * P:(t + 1) * P],
                                                wbuf[n % 2][:, k, :], start=(k == 0), stop=(k == KT - 1))
                last.then_inc(dense_ready, 1)

            for b in range(HALVES):
                n0 = UNITS * b
                pe.wait_ge(x_in, 16 * (b + 1))
                if b:
                    pe.wait_ge(ks_out, 8 * b + START)
                transposes(2 * b, hs[b])
                pe.wait_ge(tr_done, 16 * b + 8)
                if not b:
                    pe.wait_ge(tr_lo, 8)
                acts = (act_hi, act_lo) if not b else xT
                attn_br = (br_hi, br_lo) if not b else aT
                conv_br = (br_hi, br_lo) if not b else cT
                if not b:
                    pe.wait_ge(setup_done, 5)
                for u in range(2):
                    n = n0 + U_K + u
                    if b:
                        pe.wait_ge(k_ready[u], 64 * (b + 1))
                        pe.wait_ge(dense_out, n - 3)
                    half_T(n, acts, 0)
                    half_T(n, acts, 1)
                unit_tokens(n0 + U_V, acts)
                unit_T(n0 + U_Q, acts)
                pe.wait_ge(dense_out, n0 + U_Q)

                with pe.Fori(0, 2) as i:
                    for u in range(4):
                        n = n0 + U_Q + u
                        pe.wait_ge(dense_out, 4 * i + (n + 1))
                        if u % 2 == 0:
                            pe.wait_ge(keys_ready, 2 * i + (4 * b + u // 2 + 1))
                        q = stage[n % 4]
                        for t in range(TILES):
                            s = 16 * b + 2 * u + t
                            for at, h in enumerate(ORDER):
                                lo = (h % 2) * HD
                                pe.wait_ge(pT_copied, 16 * i + (2 * s + at // 2 - 1 + START))
                                nc.tensor.matmul(score_ps[at // 2][:, at % 2, :],
                                                 q[lo:lo + HD, h // 2, t * P:(t + 1) * P],
                                                 keys[lo:lo + HD, u // 2, t * P:t * P + 2 * P],
                                                 start=True, stop=True).then_inc(scores_ready, 1)
                            if t == 0:
                                begin(n + 1, 4, i)
                            half_T(n + 1, acts, t, 4, i, 0, 12)
                            for at, h in enumerate(ORDER):
                                pe.wait_ge(exp_done, 32 * i + (4 * s + at + 1 + START))
                                for c in range(2):
                                    last = nc.tensor.transpose(score_ps[at // 2][:, at % 2, c * P:(c + 1) * P],
                                                               probs[:, h, c * P:(c + 1) * P], ident[:, :])
                                if at % 2:
                                    last.then_inc(pT_ready, 1)
                            pe.wait_ge(attn_ready, 8 * i + (s + START))
                            for at, h in enumerate(ORDER):
                                pe.wait_ge(pT_copied, 16 * i + (2 * s + at // 2 + 1 + START))
                                for c in range(2):
                                    last = nc.tensor.matmul(o_ps[:, h, :], pT[:, at, c * P:(c + 1) * P],
                                                            v[:, t + c, bass.ds(i * (2 * HD) + (u // 2) * HD, HD)],
                                                            start=(c == 0), stop=(c == 1))
                            last.then_inc(o_ready, 1)
                            half_T(n + 1, acts, t, 4, i, 12, KT)
                            pe.wait_ge(attn_ready, 8 * i + (s + 1 + START))
                            if b:
                                pe.wait_ge(aT_done, 8 * i + (s + START))
                            else:
                                pe.wait_ge(br_split, 8 * i + (s + START))
                            for c in range(2):
                                last = nc.tensor.transpose(oT_ps[:, c * P:(c + 1) * P], attn[:, c * P:(c + 1) * P],
                                                           ident[:, :])
                            last.then_inc(oT_ready, 1)

                pe.wait_ge(aT_done, 16 * (b + 1) + START)
                if not b:
                    pe.wait_ge(br_split, 16 + START)
                for c in range(1, 4):
                    unit_T(n0 + U_GA + c, attn_br if c % 2 else acts)
                with pe.Fori(0, 3) as i:
                    for c in range(4):
                        unit_T(n0 + U_GA + 4 + c, attn_br if c % 2 else acts, 4, i)

                with pe.Fori(0, 6) as i:
                    for c in range(4):
                        unit_T(n0 + U_CONV + c, acts, 4, i)

                unit_T(n0 + U_GC, acts)
                pe.wait_ge(conv_step, conv0[b + 1] + START)
                for c in range(1, 4):
                    unit_T(n0 + U_GC + c, conv_br if c % 2 else acts)
                with pe.Fori(0, 3) as i:
                    for c in range(4):
                        unit_T(n0 + U_GC + 4 + c, conv_br if c % 2 else acts, 4, i)

                pe.wait_ge(gate_step, 24 * (b + 1) + START)
                if not b:
                    pe.wait_ge(m_lo, 8)
                with pe.Fori(0, 2) as i:
                    for c in range(4):
                        unit_tokens(n0 + U_OUT + c, acts if not b else mT, 4, i)

                transposes(2 * b + 1, hs[b])
                pe.wait_ge(tr_done, 16 * b + 16)
                if not b:
                    pe.wait_ge(tr_lo, 16)
                with pe.Fori(0, 2) as i:
                    for c in range(4):
                        n = n0 + U_PQ + c
                        unit_T(n, acts, 4, i)
                        pe.wait_ge(dense_out, 4 * i + (n + 1))
                        pe.wait_ge(ks_out, 4 * i + (8 * b + c - 1 + START))
                        for t in range(TILES):
                            for a in range(2):
                                last = nc.tensor.matmul(score_ps[c % 2][:, t, a * NK:(a + 1) * NK],
                                                        stage[n % 4][:, a, t * P:(t + 1) * P],
                                                        skT[:, bass.ds(8 * i + 2 * c + a, 1), :], start=True, stop=True)
                        last.then_inc(ks_ready, 1)

        @block.vector
        def _(dve):
            V = nc.vector

            class Rows:

                def __init__(self, on, t, part, per, i, base=0):
                    self.on, self.t, self.part, self.per, self.i, self.at = on, t, part, per, i, base

                def use(self, count):
                    if not self.on:
                        return
                    t, per, i = self.t, self.per, self.i
                    for _ in range(count):
                        slot = self.at % RING
                        g = t * ROWS + self.part * SLOTS + self.at
                        dve.wait_ge(row_in[slot], (16 * per // RING) * i + 16 * (g // RING + 1))
                        col = per * i + self.at
                        if self.part == 0:
                            V.scalar_tensor_tensor(out=row[slot][:, :], in0=row[slot][:, :], scalar=1.0,
                                                   in1=hs[t // TILES][:, t % TILES, :], op0=ALU.mult, op1=ALU.mult,
                                                   accum_out=dots[:, bass.ds(col, 1)]).then_inc(row_used, 1)
                        else:
                            dve.wait_ge(row_used, per * i + (g + START))
                            V.scalar_tensor_tensor(out=y[:, :], in0=row[slot][:, :], scalar=wgt[:, bass.ds(col, 1)],
                                                   in1=y[:, :], op0=ALU.mult, op1=ALU.add).then_inc(row_used, 1)
                        self.at += 1

            def weigh(t):
                dve.wait_ge(gelu_ready, t + 1)
                V.tensor_tensor(wgt[:, :], gelu[:, :], gate[:, t // TILES, t % TILES, :], ALU.mult).then_inc(wgt_ready, 1)
                dve.wait_ge(wgt_ready, t + 1)
                dve.wait_ge(y_init, t + 1)

            def finish_tile(t):
                f = 8 * t
                dve.wait_ge(row_used, ROWS * (t + 1) + START)
                for c in range(4):
                    V.bn_stats(bst2[:, c, :], y[:, c * 512:(c + 1) * 512]).then_inc(fin_step, 1)
                dve.wait_ge(fin_step, f + 4)
                V.bn_aggr(mv2[:, :], bst2[:, :, :].rearrange("p c s -> p (c s)")).then_inc(fin_step, 1)
                dve.wait_ge(sd2_ready, t + 1)
                V.reciprocal(rstd2[:, :], sd2[:, :]).then_inc(fin_step, 1)
                dve.wait_ge(fin_step, f + 6)
                dve.wait_ge(ln2_in, 32)
                V.scalar_tensor_tensor(out=y[:, :], in0=y[:, :], scalar=mv2[:, 0:1], in1=ln2[:, 0, :],
                                       op0=ALU.subtract, op1=ALU.mult).then_inc(fin_step, 1)
                dve.wait_ge(fin_step, f + 7)
                V.scalar_tensor_tensor(out=y[:, :], in0=y[:, :], scalar=rstd2[:, :], in1=ln2[:, 1, :],
                                       op0=ALU.mult, op1=ALU.add).then_inc(fin_step, 1)

            for count in (masked, exp_done, pT_copied, attn_ready, aT_done, oT_ready, conv_step, gate_step, out_step,
                          pick_step, ks_out, row_used, br_split):
                dve.sem_inc(count, START)
            V.memset(kT[:, :, 0:P], 0.0)
            V.memset(v[:, 0, :], 0.0)
            V.memset(carry[:, :, :], 0.0)
            V.memset(eps[:, :], EPS).then_inc(const_ok, 1)
            dve.wait_ge(small_in, 64)
            V.tensor_scalar(nsink[:, :], sink[:, :], -1.0, None, ALU.mult).then_inc(nsink_ok, 1)
            dve.wait_ge(nsink_ok, 1)
            dve.wait_ge(const_ok, 1)
            dve.wait_ge(masks_ok, 7)
            dve.wait_ge(setup_done, 5)

            def split_lo(q, per=0, i=0):
                n, c = q // 2, q % 2
                if n >= UNITS:
                    return
                dve.wait_ge(w_hi_ready, (2 * per) * i + (q + 1))
                V.tensor_tensor(part_of(n, w_lo[c]), unit_half(n, c), part_of(n, w_hi[c]).bitcast(F32), ALU.subtract
                                ).then_inc(w_lo_ready, 1)

            def split_transposes(call):
                for r in range(8):
                    blk = slice(2 * r, 2 * r + 2)
                    dve.wait_ge(tr_done, 8 * call + r + 1)
                    V.tensor_tensor(act_lo[:, blk, :], score_ps[r % 2][:, :, :],
                                    act_hi[:, blk, :].bitcast(F32), ALU.subtract).then_inc(tr_lo, 1)

            for b in range(HALVES):
                rows_on = b == 1 and OVERLAP
                first = b == 0
                if first:
                    split_transposes(0)
                    for q in range(9):
                        split_lo(q)
                else:
                    Rows(rows_on, 0, 0, 0, 0).use(16)
                with dve.Fori(0, 2) as i:
                    rows = Rows(rows_on, 0, 0, 56, i, base=16)
                    for u in range(4):
                        for t in range(TILES):
                            s = 16 * b + 2 * u + t
                            for at, h in enumerate(ORDER):
                                dve.wait_ge(scores_ready, 32 * i + (4 * s + 2 * (at // 2) + 2))
                                dve.wait_ge(exp_done, 32 * i + (4 * s + at - 3 + START))
                                dve.sem_inc(went_on, 1)
                                V.tensor_tensor_reduce(out=sm[:, h, :], in0=score_ps[at // 2][:, at % 2, :],
                                                       in1=mask[:, 1 if b or t else 0, :], scale=-(HD ** -0.5),
                                                       scalar=3.0e38, op0=ALU.add, op1=ALU.min,
                                                       accum_out=nmax[:, h:h + 1]).then_inc(masked, 1)
                                rows.use(1)
                            dve.wait_ge(masked, 32 * i + (4 * (s + 1) + START))
                            heads = bass.ds(16 * i + 4 * u, 4)
                            V.tensor_tensor(nmx[:, :], nmax[:, :], nsink[:, heads], ALU.min).then_inc(nmax_ready, 1)
                            dve.wait_ge(nmax_ready, 8 * i + (s + 1))
                            V.tensor_tensor(sarg[:, :], nmx[:, :], sink[:, heads], ALU.add).then_inc(sarg_ready, 1)
                            dve.wait_ge(esink_ready, 8 * i + (s + 1))
                            V.tensor_tensor(den[:, :], rowsum[:, :], esink[:, :], ALU.add).then_inc(den_ready, 1)
                            dve.wait_ge(den_ready, 8 * i + (s + 1))
                            V.reciprocal(rden[:, :], den[:, :]).then_inc(rden_ready, 1)
                            if first:
                                split_lo(2 * (UNITS * b + U_Q + u + 1) + t + 1, 4, i)
                            rows.use(2)
                            dve.wait_ge(rden_ready, 8 * i + (s + 1))
                            dve.wait_ge(o_ready, 8 * i + (s + 1))
                            dve.wait_ge(oT_ready, 8 * i + (s + START))
                            V.tensor_tensor(attn.rearrange("p (h d) -> p h d", h=4),
                                            o_ps[:, :, :],
                                            rden[:, :].unsqueeze(2).to_broadcast([P, 4, HD]), ALU.mult
                                            ).then_inc(attn_ready, 1)
                            rows.use(1)
                            if first:
                                to = (slice(None), bass.ds(8 * i + 2 * u, 2), slice(t * P, (t + 1) * P))
                                dve.wait_ge(aT_done, 8 * i + (s + 1 + START))
                                V.tensor_tensor(br_lo[to], oT_ps[:, :].rearrange("p (c t) -> p c t", c=2),
                                                br_hi[to].bitcast(F32), ALU.subtract).then_inc(br_split, 1)
                if rows_on:
                    weigh(0)

                with dve.Fori(0, 4) as i:
                    rows = Rows(rows_on, 0, 1, 12, i)
                    for g in range(2):
                        n = UNITS * b + U_GA + 2 * g
                        if first:
                            split_lo(2 * n + 3, 4, i)
                            split_lo(2 * n + 4, 4, i)
                        rows.use(3)
                        dve.wait_ge(dense_out, 4 * i + (n + 2))
                        V.tensor_tensor(mT[:, bass.ds(4 * i + 2 * g, 2), :], stage[n % 4][:, :, :],
                                        stage[(n + 1) % 4][:, :, :], ALU.mult).then_inc(gate_step, 1)
                        rows.use(3)
                        if first:
                            split_lo(2 * n + 5, 4, i)
                            split_lo(2 * n + 6, 4, i)

                cs = CONV_STEPS[b]
                with dve.Fori(0, 2) as i:
                    rows = Rows(rows_on, 0, 1, 40, i, base=48)
                    for c in range(4):
                        n = UNITS * b + U_CONV + 3 * c
                        f = conv0[b] + cs * c
                        sB, sC, sH = stage[n % 4], stage[(n + 1) % 4], stage[(n + 2) % 4]
                        ch = bass.ds(8 * i + 2 * c, 2)

                        def step(k):
                            dve.wait_ge(conv_step, (4 * cs) * i + (f + k + START))

                        if first:
                            for q in range(3, 8):
                                split_lo(2 * n + q, 12, i)
                        step(0)
                        dve.sem_inc(went_on, 1)
                        V.tensor_copy(uconv[:, :, 0:2], carry[:, ch, :]).then_inc(conv_step, 1)
                        dve.wait_ge(dense_out, 12 * i + (n + 3))
                        V.tensor_tensor(uconv[:, :, 2:2 + HALF], sC[:, :, :], sH[:, :, :], ALU.mult
                                        ).then_inc(conv_step, 1)
                        rows.use(4)
                        step(2)
                        dve.sem_inc(went_on, 1)
                        V.tensor_copy(carry[:, ch, :], uconv[:, :, HALF:HALF + 2]).then_inc(conv_step, 1)
                        for ct in range(2):
                            last = V.tensor_scalar(sC[:, ct, :], uconv[:, ct, 0:HALF],
                                                   vecs[:, bass.ds(8 * i + (32 + 2 * c + ct), 1)], None, ALU.mult)
                        last.then_inc(conv_step, 1)
                        if first:
                            split_lo(2 * n + 8, 12, i)
                        for tap in (1, 2):
                            step(3 + tap)
                            for ct in range(2):
                                last = V.scalar_tensor_tensor(
                                    out=sC[:, ct, :], in0=uconv[:, ct, tap:tap + HALF],
                                    scalar=vecs[:, bass.ds(8 * i + (32 + 16 * tap + 2 * c + ct), 1)],
                                    in1=sC[:, ct, :], op0=ALU.mult, op1=ALU.add)
                            last.then_inc(conv_step, 1)
                        step(6)
                        if first:
                            V.tensor_tensor(sC[:, :, :], sC[:, :, :], sB[:, :, :], ALU.mult).then_inc(conv_step, 1)
                            step(7)
                            V.tensor_scalar(br_hi[:, ch, :], sC[:, :, :], 1.0, None, ALU.mult).then_inc(conv_step, 1)
                            step(8)
                            V.tensor_tensor(br_lo[:, ch, :], sC[:, :, :], br_hi[:, ch, :].bitcast(F32), ALU.subtract
                                            ).then_inc(conv_step, 1)
                        else:
                            V.tensor_tensor(cT[:, ch, :], sC[:, :, :], sB[:, :, :], ALU.mult).then_inc(conv_step, 1)
                        rows.use(6)
                if rows_on:
                    finish_tile(0)

                def split_m_lo(r):
                    blk = slice(2 * r, 2 * r + 2)
                    dve.wait_ge(m_hi, r + 1)
                    V.tensor_tensor(act_lo[:, blk, :], mT[:, blk, :], act_hi[:, blk, :].bitcast(F32), ALU.subtract
                                    ).then_inc(m_lo, 1)

                def conv_gates(i, part=0):
                    rows = Rows(rows_on, 1, 0, 32, i)
                    for g in range(2):
                        n = UNITS * b + U_GC + 12 * part + 2 * g
                        if first:
                            split_lo(2 * n + 3, 4, i)
                            if part and g:
                                for r in range(7):
                                    split_m_lo(r)
                            split_lo(2 * n + 4, 4, i)
                        rows.use(8)
                        dve.wait_ge(dense_out, 4 * i + (n + 2))
                        V.tensor_tensor(stage[n % 4][:, :, :], stage[n % 4][:, :, :],
                                        stage[(n + 1) % 4][:, :, :], ALU.mult).then_inc(gate_step, 1)
                        dve.wait_ge(gate_step, 4 * i + (24 * b + 8 + 12 * part + 2 * g + 1 + START))
                        to = mT[:, bass.ds(4 * i + (12 * part + 2 * g), 2), :]
                        V.tensor_tensor(to, to, stage[n % 4][:, :, :], ALU.add).then_inc(gate_step, 1)
                        rows.use(8)
                        if first:
                            split_lo(2 * n + 5, 4, i)
                            if not (part and g):
                                split_lo(2 * n + 6, 4, i)

                if first:
                    with dve.Fori(0, 3) as i:
                        conv_gates(i)
                    conv_gates(0, 1)
                    split_m_lo(7)
                    split_lo(2 * (U_OUT + 1))
                else:
                    with dve.Fori(0, 4) as i:
                        conv_gates(i)
                if rows_on:
                    weigh(1)

                if b:
                    dve.wait_ge(xres_in, 16)
                def add_out(i, part=0):
                    rows = Rows(rows_on, 1, 1, 28, i)
                    for c in range(4):
                        n = UNITS * b + U_OUT + 4 * part + c
                        to = hs[b][:, :, bass.ds(i * (4 * UC) + (4 * part + c) * UC, UC)]
                        dve.wait_ge(dense_out, 4 * i + (n + 1))
                        V.scalar_tensor_tensor(out=to, in0=to, scalar=ALPHA, in1=stage[n % 4][:, :, :],
                                               op0=ALU.mult, op1=ALU.add).then_inc(out_step, 1)
                        rows.use(7)
                        if c % 2:
                            dve.wait_ge(out_step, 4 * i + (8 * b + 4 * part + c + 1 + START))
                            dve.sem_inc(went_on, 1)
                            for t in range(TILES):
                                V.bn_stats(bst[:, t, bass.ds(2 * i + (2 * part + c // 2), 1), :]
                                           .rearrange("p o s -> p (o s)"),
                                           hs[b][:, t, bass.ds(i * (4 * UC) + (4 * part + c - 1) * UC, 2 * UC)]
                                           ).then_inc(stats_step, 1)
                        if first:
                            split_lo(2 * n + 3)
                            if 4 * part + c < 7:
                                split_lo(2 * n + 4)

                if first:
                    add_out(0)
                    add_out(0, 1)
                else:
                    with dve.Fori(0, 2) as i:
                        add_out(i)
                ln_rows = Rows(rows_on, 1, 1, 0, 0, base=56)
                for t in range(TILES):
                    dve.wait_ge(stats_step, 10 * b + 8)
                    V.bn_aggr(mv[:, t, :], bst[:, t, :, :].rearrange("p c s -> p (c s)")).then_inc(stats_step, 1)
                ln_rows.use(1)
                dve.wait_ge(sd_ready, b + 1)
                V.reciprocal(rstd[:, :], sd[:, :]).then_inc(ln_step, 1)
                dve.wait_ge(ln_step, 5 * b + 1)
                dve.wait_ge(ln1_in, 32 * (b + 1))
                for c in range(2):
                    part_c = slice(c * (D // 2), (c + 1) * (D // 2))
                    for t in range(TILES):
                        V.scalar_tensor_tensor(out=hs[b][:, t, part_c], in0=hs[b][:, t, part_c], scalar=mv[:, t, 0:1],
                                               in1=ln1[:, 0, part_c], op0=ALU.subtract, op1=ALU.mult
                                               ).then_inc(ln_step, 1)
                    ln_rows.use(1)
                    for t in range(TILES):
                        dve.wait_ge(ln_step, 5 * b + 2 + 2 * c + t)
                        V.scalar_tensor_tensor(out=hs[b][:, t, part_c], in0=hs[b][:, t, part_c], scalar=rstd[:, t:t + 1],
                                               in1=ln1[:, 1, part_c], op0=ALU.mult, op1=ALU.add).then_inc(h_ready, 1)
                    ln_rows.use(1)
                ln_rows.use(3)

                if first:
                    split_transposes(1)
                    split_lo(2 * (U_PQ + 1))

                def pick(i, part=0):
                    rows = Rows(rows_on, 1, 1, 24, i, base=SLOTS // 2)
                    for c in range(4):
                        n = UNITS * b + U_PQ + 4 * part + c
                        f = 12 * (8 * b + 4 * part + c)
                        sc = ks[:, c % 2, :, :, :]
                        both = [(t, a) for t in range(TILES) for a in range(2)]

                        def step(k):
                            dve.wait_ge(pick_step, 48 * i + (f + k + START))
                            dve.sem_inc(went_on, 1)

                        rows.use(2)
                        dve.wait_ge(ks_out, 4 * i + (8 * b + 4 * part + c + 1 + START))
                        dve.sem_inc(went_on, 1)
                        for t, a in both:
                            last = V.max(tops[:, t, a, 0:8], sc[:, t, a, :])
                        last.then_inc(pick_step, 1)
                        step(1)
                        for t, a in both:
                            V.max_index(topi[:, t, a, 0:8], tops[:, t, a, 0:8], sc[:, t, a, :])
                        for t, a in both:
                            last = V.match_replace(ksw[:, t, a, :], tops[:, t, a, 0:8], sc[:, t, a, :], LOWEST)
                        last.then_inc(pick_step, 1)
                        rows.use(2)
                        step(2)
                        for t, a in both:
                            last = V.max(tops[:, t, a, 8:16], ksw[:, t, a, :])
                        last.then_inc(pick_step, 1)
                        step(3)
                        for t, a in both:
                            last = V.max_index(topi[:, t, a, 8:16], tops[:, t, a, 8:16], ksw[:, t, a, :])
                        last.then_inc(pick_step, 1)
                        for t in range(TILES):
                            last = V.tensor_tensor(cand[:, t, :].rearrange("p (a b) -> p a b", a=TOPK),
                                                   tops[:, t, 0, :].unsqueeze(2).to_broadcast([P, TOPK, TOPK]),
                                                   tops[:, t, 1, :].unsqueeze(1).to_broadcast([P, TOPK, TOPK]), ALU.add)
                        last.then_inc(pick_step, 1)
                        rows.use(2)
                        step(5)
                        for t in range(TILES):
                            last = V.max(bests[:, t, 0:8], cand[:, t, :])
                        last.then_inc(pick_step, 1)
                        step(6)
                        for t in range(TILES):
                            V.max_index(bestp[:, t, 0:8], bests[:, t, 0:8], cand[:, t, :])
                        for t in range(TILES):
                            last = V.match_replace(candw[:, t, :], bests[:, t, 0:8], cand[:, t, :], LOWEST)
                        last.then_inc(pick_step, 1)
                        step(7)
                        for t in range(TILES):
                            last = V.max(bests[:, t, 8:16], candw[:, t, :])
                        last.then_inc(pick_step, 1)
                        step(8)
                        for t in range(TILES):
                            last = V.max_index(bestp[:, t, 8:16], bests[:, t, 8:16], candw[:, t, :])
                        last.then_inc(pick_step, 1)
                        V.tensor_copy(best[:, :, bass.ds(4 * i + (4 * part + c), 1), :].rearrange("p t o k -> p (t o) k"), bests
                                      ).then_inc(pick_step, 1)
                        step(9)
                        V.tensor_scalar(posab[:, :, 0, :], bestp, 4, None, ALU.logical_shift_right)
                        V.tensor_scalar(posab[:, :, 1, :], bestp, 15, None, ALU.bitwise_and).then_inc(pick_step, 1)
                        step(11)
                        fo = found[:, :, bass.ds(4 * i + (4 * part + c), 1), :].rearrange("p t o k -> p (t o) k")
                        V.tensor_copy(fo[:, :, 0:32], posab.rearrange("p t a k -> p t (a k)"))
                        V.tensor_copy(fo[:, :, 32:64], topi.rearrange("p t a k -> p t (a k)")).then_inc(pick_step, 1)
                        step(12)

                if first:
                    pick(0)
                    pick(0, 1)
                else:
                    with dve.Fori(0, 2) as i:
                        pick(i)

                f = 14 * b
                V.tensor_tensor(gate[:, b, :, :].rearrange("p t (h k) -> p (t h) k", h=PH),
                                best[:, :, :, :].rearrange("p t h k -> p (t h) k"),
                                best[:, :, :, 0:1].rearrange("p t h k -> p (t h) k").to_broadcast([P, TILES * PH, TOPK]),
                                ALU.subtract).then_inc(gather_step, 1)
                k = 1
                rows = Rows(rows_on, 1, 1, 0, 0, base=SLOTS - 16)
                for t in range(TILES):
                    for a, key in ((0, key0), (1, key1)):
                        pos = found[:, t, :, a * TOPK:(a + 1) * TOPK].unsqueeze(3).to_broadcast([P, PH, TOPK, TOPK])
                        num = found[:, t, :, (2 + a) * TOPK:(3 + a) * TOPK].unsqueeze(2).to_broadcast([P, PH, TOPK, TOPK])
                        if k > 1:
                            dve.wait_ge(gather_step, f + k)
                        V.tensor_tensor(onehot, pos, iota[:, :].unsqueeze(1).unsqueeze(1).to_broadcast([P, PH, TOPK, TOPK]),
                                        ALU.is_equal).then_inc(gather_step, 1)
                        k += 1
                        rows.use(2)
                        dve.wait_ge(gather_step, f + k)
                        V.tensor_tensor(onehot, onehot, num, ALU.mult).then_inc(gather_step, 1)
                        k += 1
                        dve.wait_ge(gather_step, f + k)
                        V.tensor_reduce(key.rearrange("p (h k) -> p h k", h=PH), onehot, AX.X, ALU.add
                                        ).then_inc(gather_step, 1)
                        k += 1
                        rows.use(2)
                    dve.wait_ge(gather_step, f + k)
                    V.scalar_tensor_tensor(out=expert[:, b, t, :], in0=key0, scalar=float(NK), in1=key1,
                                           op0=ALU.mult, op1=ALU.add).then_inc(expert_ready, 1)
                dve.wait_ge(gexp_ready, b + 1)
                gv = gate[:, b, :, :].rearrange("p t (h k) -> p (t h) k", h=PH)
                V.tensor_reduce(gsum[:, :, :].rearrange("p t h -> p (t h)"), gv, AX.X, ALU.add).then_inc(gather_step, 1)
                dve.wait_ge(gather_step, f + 14)
                V.reciprocal(grec[:, :, :], gsum[:, :, :]).then_inc(gate_norm, 1)
                dve.wait_ge(gate_norm, 2 * b + 1)
                V.tensor_tensor(gv, gv, grec[:, :, :].rearrange("p t h -> p (t h)").unsqueeze(2)
                                .to_broadcast([P, TILES * PH, TOPK]), ALU.mult).then_inc(gate_norm, 1)
                dve.wait_ge(gate_norm, 2 * b + 2)
                if rows_on:
                    finish_tile(1)
                if not OVERLAP or b == 1:
                    for t in range(b * TILES, (b + 1) * TILES):
                        for part in range(2):
                            if part:
                                weigh(t)
                            with dve.Fori(0, 8) as i:
                                Rows(True, t, part, 16, i).use(16)
                        finish_tile(t)


_OUTS = [((1, SEQ, D), 'float32')]
_INS = ["x", "w_in", "b_gate", "sinks", "conv_w", "w_attn_out", "w_conv_out", "w_o", "ln1_g", "ln1_b",
        "peer_w_q", "peer_sub_keys", "peer_u", "peer_v", "ln2_g", "ln2_b"]


def kernel(**inputs):
    import numpy as _np
    import concourse.bacc as _bacc
    from concourse import mybir as _mybir
    from concourse.bass_utils import run_bass_kernel_spmd as _run

    nc = _bacc.Bacc("TRN2", target_bir_lowering=False, num_devices=1)
    arrays, args = {}, []
    for name in _INS:
        a = _np.ascontiguousarray(inputs[name])
        arrays[f"in_{name}_dram"] = a
        args.append(nc.dram_tensor(f"in_{name}_dram", a.shape, _mybir.dt.from_np(a.dtype), kind="ExternalInput").ap())
    for i, (shape, dtype) in enumerate(_OUTS):
        dt = _mybir.dt.from_np(_np.dtype(dtype))
        args.append(nc.dram_tensor(f"out_{i}_dram", shape, dt, kind="ExternalOutput").ap())
    build(nc, *args)
    r = _run(nc, [arrays], core_ids=[0])
    return r.results[0]["out_0_dram"]
```
